# Optimizing a Trainium2 kernel written in Bass

```python
import jax, jax.numpy as jnp
from jax import lax
import numpy as np

D_MODEL = 1024
BATCH = 1
SEQ = 2048
DEPTH = 1
DEC_BATCH = 8
DEC_SEQ = 4
PAST_LEN = 16384
PAGE_SIZE = 128

N_META = 16
W_A = D_MODEL // 2
W_B = D_MODEL - W_A
A_HEADS = 8
A_HEAD_DIM = W_A // A_HEADS
CONV_W = 4
RG_C = 8.0
B_HEADS = 4
B_DK = W_B // B_HEADS
B_DV = W_B // B_HEADS
CHUNK = 64
D_FF = 4 * D_MODEL
IN_COLS = 2 * W_A + 4 * W_B
EPS = 1e-6
F_MIN = 1e-30

kernel_name = "hymba_rglru_hgrn2_decoder_step"

def _rms(x):
    x32 = x.astype(jnp.float32)
    return x32 * lax.rsqrt(jnp.mean(x32 * x32, axis=-1, keepdims=True) + EPS)

def _rmsnorm(x, g):
    return (_rms(x) * g.astype(jnp.float32)).astype(x.dtype)

def _lin_combine(c1, c2):
    a1, b1 = c1
    a2, b2 = c2
    return a1 * a2, a2 * b1 + b2

def _hgrn2_chunk(S, q, k, v, logf):
    C = q.shape[2]
    b = jnp.cumsum(logf, axis=2)
    inter = jnp.einsum('bhck,bhkv->bhcv', q * jnp.exp(b), S)
    diff = b[:, :, :, None, :] - b[:, :, None, :, :]
    mask = jnp.tril(jnp.ones((C, C), dtype=bool))[:, :, None]
    decay = jnp.exp(jnp.where(mask, diff, 0.0)) * mask.astype(diff.dtype)
    A = jnp.einsum('bhtk,bhtsk,bhsk->bhts', q, decay, k)
    intra = jnp.einsum('bhts,bhsv->bhtv', A, v)
    b_last = b[:, :, -1:, :]
    S_new = S * jnp.exp(b_last[:, :, 0, :])[..., None] + jnp.einsum(
        'bhsk,bhsv->bhkv', k * jnp.exp(b_last - b), v)
    return S_new, inter + intra

def _hgrn2(q, k, v, logf, S0, first_len):
    Bn, H, T, _ = q.shape
    S, o_first = _hgrn2_chunk(S0, q[:, :, :first_len], k[:, :, :first_len],
                              v[:, :, :first_len], logf[:, :, :first_len])
    rest = T - first_len
    if rest == 0:
        return o_first, S
    n = rest // CHUNK

    def split(z):
        return jnp.moveaxis(z[:, :, first_len:].reshape(Bn, H, n, CHUNK, z.shape[-1]), 2, 0)

    S, o_rest = lax.scan(lambda s, xs: _hgrn2_chunk(s, *xs), S,
                         (split(q), split(k), split(v), split(logf)))
    o_rest = jnp.moveaxis(o_rest, 0, 2).reshape(Bn, H, rest, v.shape[-1])
    return jnp.concatenate([o_first, o_rest], axis=2), S

def _mixer(hn, conv_buf, h0, S0, w_in, conv_w, conv_b, w_ra, b_ra, w_rx, b_rx,
           lam, lb, gn, w_out, first_len):
    Bn, T, _ = hn.shape
    f32 = jnp.float32
    u = (hn @ w_in).astype(f32)
    xa, ga, qb, fb, ib, gb = jnp.split(
        u, [W_A, 2 * W_A, 2 * W_A + W_B, 2 * W_A + 2 * W_B, 2 * W_A + 3 * W_B], axis=-1)
    xpad = jnp.concatenate([conv_buf.astype(f32), xa], axis=1)
    cw = conv_w.astype(f32)
    xc = conv_b.astype(f32) + sum(xpad[:, j:j + T] * cw[j] for j in range(CONV_W))
    new_conv = xpad[:, T:]
    xh = xc.reshape(Bn, T, A_HEADS, A_HEAD_DIM)
    r = jax.nn.sigmoid(jnp.einsum('bthi,hij->bthj', xh, w_ra.astype(f32)) + b_ra).reshape(Bn, T, W_A)
    ig = jax.nn.sigmoid(jnp.einsum('bthi,hij->bthj', xh, w_rx.astype(f32)) + b_rx).reshape(Bn, T, W_A)
    log_a = -RG_C * r * jax.nn.softplus(-lam.astype(f32))
    a = jnp.exp(log_a)
    bt = jnp.sqrt(-jnp.expm1(2.0 * log_a)) * ig * xc
    bt = bt.at[:, 0].add(a[:, 0] * h0.astype(f32))
    _, hs = lax.associative_scan(_lin_combine, (a, bt), axis=1)
    y_a = hs * jax.nn.gelu(ga)
    h_new = hs[:, -1]
    def heads(z):
        return z.reshape(Bn, T, B_HEADS, -1).transpose(0, 2, 1, 3)
    q = heads(jax.nn.silu(qb)) * (B_DK ** -0.5)
    lbh = lb.astype(f32).reshape(B_HEADS, 1, B_DK)
    fpre = heads(fb)
    f = lbh + (1.0 - lbh) * jax.nn.sigmoid(fpre)
    logf = jnp.log(jnp.maximum(f, F_MIN))
    k = (1.0 - lbh) * jax.nn.sigmoid(-fpre)
    v = heads(ib)
    o, S_new = _hgrn2(q, k, v, logf, S0.astype(f32), first_len)
    o = o.transpose(0, 2, 1, 3)
    o = _rms(o) * gn.astype(f32) * jax.nn.silu(gb.reshape(Bn, T, B_HEADS, B_DV))
    y = jnp.concatenate([y_a, o.reshape(Bn, T, W_B)], axis=-1)
    return (y.astype(hn.dtype) @ w_out), new_conv, h_new, S_new

def setup_inputs(seed: int = 0) -> dict:
    key = jax.random.key(seed)
    ks = jax.random.split(key, 24)
    nrm = jax.random.normal
    f32 = jnp.float32
    u_a = jax.random.uniform(ks[13], (DEPTH, W_A), f32, 0.9, 0.999)
    return {
        "x_prompt": nrm(ks[0], (BATCH, SEQ, D_MODEL), f32),
        "x_sample": nrm(ks[1], (DEC_BATCH, DEC_SEQ, D_MODEL), f32),
        "state_rglru_h": 0.5 * nrm(ks[2], (DEPTH, DEC_BATCH, W_A), f32),
        "state_rglru_conv": nrm(ks[3], (DEPTH, DEC_BATCH, CONV_W - 1, W_A), f32),
        "state_hgrn2": 0.3 * nrm(ks[4], (DEPTH, DEC_BATCH, B_HEADS, B_DK, B_DV), f32),
        "meta_tokens": nrm(ks[5], (N_META, D_MODEL), f32),
        "ln_mix": 1.0 + 0.02 * nrm(ks[6], (DEPTH, D_MODEL), f32),
        "w_in": nrm(ks[7], (DEPTH, D_MODEL, IN_COLS), f32) * D_MODEL ** -0.5,
        "conv_w": nrm(ks[8], (DEPTH, CONV_W, W_A), f32) * CONV_W ** -0.5,
        "conv_b": 0.02 * nrm(ks[9], (DEPTH, W_A), f32),
        "w_rg_a": nrm(ks[10], (DEPTH, A_HEADS, A_HEAD_DIM, A_HEAD_DIM), f32) * A_HEAD_DIM ** -0.5,
        "b_rg_a": 0.02 * nrm(ks[11], (DEPTH, A_HEADS, A_HEAD_DIM), f32),
        "w_rg_x": nrm(ks[12], (DEPTH, A_HEADS, A_HEAD_DIM, A_HEAD_DIM), f32) * A_HEAD_DIM ** -0.5,
        "b_rg_x": 0.02 * nrm(ks[14], (DEPTH, A_HEADS, A_HEAD_DIM), f32),
        "rg_lambda": jnp.log(u_a / (1.0 - u_a)),
        "hgrn_lb": 0.5 * nrm(ks[15], (DEPTH, W_B), f32),
        "hgrn_norm": 1.0 + 0.02 * nrm(ks[16], (DEPTH, B_DV), f32),
        "w_out": nrm(ks[17], (DEPTH, D_MODEL, D_MODEL), f32) * D_MODEL ** -0.5,
        "ln_mlp": 1.0 + 0.02 * nrm(ks[18], (DEPTH, D_MODEL), f32),
        "w_up": nrm(ks[19], (DEPTH, D_MODEL, D_FF), f32) * D_MODEL ** -0.5,
        "w_down": nrm(ks[20], (DEPTH, D_FF, D_MODEL), f32) * D_FF ** -0.5,
        "ln_final": 1.0 + 0.02 * nrm(ks[21], (D_MODEL,), f32),
    }

def reference(x_prompt, x_sample, state_rglru_h, state_rglru_conv, state_hgrn2,
              meta_tokens, ln_mix, w_in, conv_w, conv_b, w_rg_a, b_rg_a, w_rg_x, b_rg_x,
              rg_lambda, hgrn_lb, hgrn_norm, w_out, ln_mlp, w_up, w_down, ln_final):
    f32 = jnp.float32
    lbs = jax.nn.softmax(hgrn_lb.astype(f32), axis=0)
    lb_all = jnp.clip(jnp.cumsum(lbs, axis=0) - lbs[0], 0.0, 1.0)

    meta = jnp.broadcast_to(meta_tokens.astype(x_prompt.dtype), (BATCH, N_META, D_MODEL))
    xp = jnp.concatenate([meta, x_prompt], axis=1)
    xs = x_sample
    p_conv = jnp.zeros((BATCH, CONV_W - 1, W_A), f32)
    p_h = jnp.zeros((BATCH, W_A), f32)
    p_S = jnp.zeros((BATCH, B_HEADS, B_DK, B_DV), f32)

    ph_l, pc_l, pS_l, sh_l, sc_l, sS_l = [], [], [], [], [], []
    for l in range(DEPTH):
        wl = (w_in[l], conv_w[l], conv_b[l], w_rg_a[l], b_rg_a[l], w_rg_x[l], b_rg_x[l],
              rg_lambda[l], lb_all[l], hgrn_norm[l], w_out[l])
        mp, cp, hp, Sp = _mixer(_rmsnorm(xp, ln_mix[l]), p_conv, p_h, p_S, *wl, N_META)
        ms, cs, hs, Ss = _mixer(_rmsnorm(xs, ln_mix[l]), state_rglru_conv[l], state_rglru_h[l],
                                state_hgrn2[l], *wl, xs.shape[1])
        xp = xp + mp
        xs = xs + ms
        pn = _rmsnorm(xp, ln_mlp[l])
        xp = xp + jnp.square(jax.nn.relu(pn @ w_up[l])) @ w_down[l]
        sn = _rmsnorm(xs, ln_mlp[l])
        xs = xs + jnp.square(jax.nn.relu(sn @ w_up[l])) @ w_down[l]
        ph_l.append(hp); pc_l.append(cp); pS_l.append(Sp)
        sh_l.append(hs); sc_l.append(cs); sS_l.append(Ss)

    y_prompt = _rmsnorm(xp, ln_final)[:, N_META:]
    y_sample = _rmsnorm(xs, ln_final)
    return (y_prompt, y_sample, jnp.stack(ph_l), jnp.stack(pc_l), jnp.stack(pS_l),
            jnp.stack(sh_l), jnp.stack(sc_l), jnp.stack(sS_l))


_drawn_inputs = setup_inputs


def setup_inputs(seed=0):
    import zlib

    import numpy as np

    out = dict(_drawn_inputs(seed))
    spreads = {}
    factors = {'meta_tokens': 4.618,
     'b_rg_a': 8.0,
     'b_rg_x': 8.0,
     'hgrn_norm': 6.452,
     'ln_mlp': 3.385,
     'ln_final': 2.757}
    for name, (base, spread) in spreads.items():
        noise = np.random.default_rng([zlib.crc32(name.encode()), seed]).standard_normal(out[name].shape)
        drawn = base * np.exp(spread * noise) if base else spread * noise
        out[name] = __import__('jax').numpy.asarray(drawn.astype(out[name].dtype))
    for name, factor in factors.items():
        out[name] = (out[name] * factor).astype(out[name].dtype)
    return out
```

```python
from contextlib import ExitStack

import numpy as np

import concourse.bass as bass
from concourse import mybir

F32 = mybir.dt.float32
F32R = mybir.dt.float32r
I32 = mybir.dt.int32
ALU = mybir.AluOpType
ACT = mybir.ActivationFunctionType

P = 128
DM = 1024
KB = DM // P
META, SEQ = 16, 2048
NSEQ, SLEN = 8, 4
NSMP = NSEQ * SLEN
HEADS = 4
CH = 128
LEVELS = 7
TAPS = 4
FF_GROUPS = 4
EPS = 1e-6
F_MIN = 1e-30
QSCALE = float(P) ** -0.5

TH = [1024, META + SEQ - 1024 + NSMP]
NP = [1024, META + SEQ - 1024]
TAIL = NP[1] - 1024
T8 = TAIL + NSMP
TMAX = TH[1]
TILES = [[(0, 512), (512, 512)], [(0, 358), (358, 358), (716, 356)]]
NT = [2, 3]
NCH = 8
BLOCKS = 96
V, G, XA, F, Q = range(5)
GA0, OUT0, MLP0 = 20, 24, 32
OUT_ORDER = [0, 1, 2, 4, 5, 6, 7, 3]

PC = {}
_at = 0
for _name, _n in (("ln_mix", 8), ("ln_mlp", 8), ("ln_final", 8), ("conv_w", 16), ("conv_b", 4), ("b_ra", 4),
                  ("b_rx", 4), ("lam", 4), ("lb", 4), ("gn", 1)):
    PC[_name] = _at
    _at += _n
NPARAM = _at


def unit_no(p, blk, t):
    return p * BLOCKS * NT[0] + blk * NT[p] + t


def sum_no(p, m, t):
    return (KB - 1) * NT[0] * p + (m - 1) * NT[p] + t + 1


def post_no(p, kind, i, t):
    base = p * 16 * NT[0]
    return base + (i * 3 + kind) * NT[p] + t if kind < 3 else base + (12 + i) * NT[p] + t


RG_STEPS = [
    ["hist", "c0", "c1", "c2", "c3", "u", "a", "v", "igx", "bt", "scan", "hprev", "xhist"],
    ["hist", "c0", "c1", "c2", "c3", "sc0", "sc1", "sc2", "sc3", "u", "a", "v", "igx", "bt", "fold", "foldadd",
     "cut", "scan", "hprev", "xhist", "hout", "ncs"],
]


def rg_at(p, i, name):
    return p * 4 * len(RG_STEPS[0]) + i * len(RG_STEPS[p]) + RG_STEPS[p].index(name) + 1


S_STEPS = [["s0", "s1", "s2", "s3", "s5", "s6", "s7"],
           ["vm", "s0", "s1", "s2", "s3", "s5", "s6", "s7", "smul"]]


def s_at(p, i, name):
    return p * 4 * len(S_STEPS[0]) + i * len(S_STEPS[p]) + S_STEPS[p].index(name) + 1


O_STEPS = 3
PREP_STEPS = 25
PIECES = ["VT", "D"] + [f"L{l}" for l in range(1, 8)] + ["KT", "U", "O", "SS"]
SLOTS = [dict(zip(range(13), PIECES)),
         dict(zip([0, 2, 3, 5, 6, 8, 9, 11, 12, 13, 14, 16, 18], PIECES))]
GATE_SLOT = [15, 22]
RS_SLOT = [3, 7]
NF_SLOT = 3


def schedule(p):
    out = []
    for i in range(HEADS + 1):
        blks = [5 * i + b for b in range(5)] if i < HEADS else [GA0 + c for c in range(4)]
        s = 0
        for blk in blks:
            for t in range(NT[p]):
                for half in range(2):
                    pieces = []
                    if p and i == 0 and s == NF_SLOT:
                        pieces.append(("NF", 0))
                    if i == 0 and s == RS_SLOT[p]:
                        pieces.append(("RS", 0))
                    if i >= 1 and s in SLOTS[p]:
                        pieces.append((SLOTS[p][s], i - 1))
                    if i < HEADS and s == GATE_SLOT[p]:
                        pieces.append(("GATE", i))
                    out.append((i, blk, t, half, pieces))
                    s += 1
    return out


def aux_uses(p, name):
    if name in ("RS", "N2", "NF"):
        return NT[p]
    if name == "GATE":
        return 2 * NT[p]
    if name[0] == "L":
        return 1 + (p == 1 and int(name[1]) <= 4)
    if name == "U":
        return 2 + 3 * p
    return 2 + p


def number_aux():
    at, n, seen = {}, 0, []
    for p in range(2):
        order = [(name, i) for *_, pieces in schedule(p) for name, i in pieces] + [("N2", 0)] + [("NF", 0)] * p
        for name, i in order:
            own = p
            if name == "NF":
                own = len(seen)
                seen.append(name)
            at[(own, name, i)] = n
            n += aux_uses(own, name)
    return at


AUX = number_aux()


def build(nc, ins, outs):
    (xT, wall, par_d, wra_d, wrx_d, h0_d, cs_d, ss_d, ident_d, mask_d, smask_d) = ins
    (y_d, hp_d, cp_d, sp_d, hs_d, csn_d, ssn_d) = outs

    with ExitStack() as ctx:
        def sb(name, shape, dt=F32, stack=ctx):
            return stack.enter_context(nc.sbuf_tensor(name, shape, dt))

        def sem(name):
            return ctx.enter_context(nc.semaphore(name))

        a_hi = sb("a_hi", [P, KB, TMAX], F32R)
        a_lo = sb("a_lo", [P, KB, TMAX], F32R)
        xy = sb("xy", [P, KB, TMAX])
        w_st = sb("w_st", [P, 2, DM])
        w_hi = sb("w_hi", [P, 2, DM], F32R)
        w_lo = sb("w_lo", [P, 2, DM], F32R)
        rs = sb("rs", [P, TMAX])
        tmp = sb("tmp", [P, 2, 512])
        state = sb("state", [P, HEADS, P])
        ident = sb("ident", [P, P])
        ones = sb("ones", [P, P])
        par = sb("par", [P, NPARAM])
        eps = sb("eps", [P, 1])
        sp = sb("sp", [P, 4, 4])
        lbv = sb("lbv", [P, 2, 4])
        hprev = sb("hprev", [P, 4])
        xhist = sb("xhist", [P, 4, TAPS - 1])
        w_ra = sb("w_ra", [P, 4, P])
        w_rx = sb("w_rx", [P, 4, P])
        with ExitStack() as r:
            q = sb("q", [P, TMAX], stack=r)
            k = sb("k", [P, TMAX], stack=r)
            f = sb("f", [P, TMAX], stack=r)
            v = sb("v", [P, TMAX], stack=r)
            gate = sb("gate", [P, 2, TMAX], stack=r)
            with ExitStack() as r2:
                xs = sb("xs", [P, KB, TMAX], stack=r2)
            v_tok = sb("v_tok", [P, 9, P], stack=r)
            k_tok = sb("k_tok", [P, 9, P], stack=r)
            attn = sb("attn", [P, TMAX], stack=r)
            s_in = sb("s_in", [P, 9, P], stack=r)
            s_smp = sb("s_smp", [P, NSEQ, P], stack=r)
            xpad = sb("xpad", [P, TAPS - 1 + NP[1]], stack=r)
            xc = sb("xc", [P, TMAX], stack=r)
            ta = sb("ta", [P, TMAX], stack=r)
            ea = sb("ea", [P, TMAX], stack=r)
            spad = sb("spad", [P, 4, NSEQ, TAPS - 1 + SLEN], stack=r)
            h0 = sb("h0", [P, 4, NSEQ], stack=r)
            hout = sb("hout", [P, 4, NSEQ], stack=r)
            ncs = sb("ncs", [P, 4, NSEQ, TAPS - 1], stack=r)
            fold = sb("fold", [P, NSEQ], stack=r)
            mask = sb("mask", [P, P + LEVELS * 64], I32, stack=r)
            smask = sb("smask", [T8, NSEQ], stack=r)
        b_hi = sb("b_hi", [P, KB, TMAX], F32R)
        b_lo = sb("b_lo", [P, KB, TMAX], F32R)
        ig = k_tok[:, :, :].rearrange("p c d -> p (c d)")
        ge = xc
        sq = [q, k]

        bank = [ctx.enter_context(nc.psum_tensor(f"bank{j}", [P, 512], F32)) for j in range(4)]
        aux = [ctx.enter_context(nc.psum_tensor(f"aux{j}", [P, 512], F32)) for j in range(4)]

        w_in = [sem("w_in0"), sem("w_in1")]
        w_split = sem("w_split")
        w_ready = sem("w_ready")
        unit_done = sem("unit_done")
        bank_free = [sem(f"bank_free{j}") for j in range(4)]
        aux_done = sem("aux_done")
        aux_free = [sem(f"aux_free{j}") for j in range(4)]
        const_in = sem("const_in")
        par_in = sem("par_in")
        smp_in = sem("smp_in")
        consts = sem("consts")
        prep_act = sem("prep_act")
        prep = sem("prep")
        x_in = [sem(f"x_in{b}") for b in range(KB)]
        x_hi = sem("x_hi")
        x_ready = sem("x_ready")
        x_sq = sem("x_sq")
        x_acc = sem("x_acc")
        rs_ready = sem("rs_ready")
        act_fn = sem("act_fn")
        post = sem("post")
        post_half = sem("post_half")
        zeroed = sem("zeroed")
        spread = sem("spread")
        level = sem("level")
        s_step = sem("s_step")
        s_load = sem("s_load")
        s_store = sem("s_store")
        rg_step = sem("rg_step")
        rg_act = sem("rg_act")
        o_inv = sem("o_inv")
        y_hi = sem("y_hi")
        y_ready = sem("y_ready")
        b_act = sem("b_act")
        b_lo_ready = sem("b_lo_ready")
        b_sum = sem("b_sum")
        h_sq = sem("h_sq")
        h_ready = sem("h_ready")
        f_sq = sem("f_sq")
        f_sum = sem("f_sum")
        y_out = sem("y_out")
        stored = sem("stored")
        small_out = sem("small_out")

        def evacuated(eng, u):
            eng.wait_ge(bank_free[u % 4], u // 4 + 1)

        def filled(eng, a):
            eng.wait_ge(aux_done, a + 1)

        def drained(eng, a):
            eng.wait_ge(aux_free[a % 4], a // 4 + 1)

        def col(name, j=0):
            return par[:, PC[name] + j:PC[name] + j + 1]

        def norms_before(p, which):
            return 3 * NT[0] * p + which * NT[p]

        def chunk_sets(p):
            return [(0, 4), (4, 4)] + ([(8, 1)] if p else [])

        def span(c, n=1):
            return (CH * c, CH * c + (CH * n if c < NCH else T8))

        def rows(c):
            return CH if c < NCH else T8

        block = ctx.enter_context(nc.Block())

        @block.sync
        def _(sync):
            def load(p, m, slot):
                sync.dma_start(w_st[:, slot, :], wall[m]).then_inc(w_in[slot], 16)

            for p in range(2):
                for j in range(2):
                    if p:
                        sync.wait_ge(w_ready, BLOCKS * p + j - 1)
                    load(p, j, j)
                with sync.Fori(1, BLOCKS // 2) as i:
                    for j in range(2):
                        sync.wait_ge(w_ready, 2 * i + (BLOCKS * p + j - 1))
                        load(p, 2 * i + j, j)

        @block.gpsimd
        def _(pool):
            pool.memset(ones[:, :], 1.0).then_inc(consts, 1)
            pool.memset(eps[:, :], EPS).then_inc(consts, 1)
            pool.memset(hprev[:, :], 0.0).then_inc(consts, 1)
            pool.memset(xhist[:, :, :], 0.0).then_inc(consts, 1)
            pool.memset(state[:, :, :], 0.0).then_inc(consts, 1)

            def split(slot, n):
                pool.tensor_tensor(w_hi[:, slot, :], w_st[:, slot, :], ones[:, 0:1].broadcast_to([P, DM]),
                                   ALU.mult).then_inc(w_split, 1)
                pool.wait_ge(w_split, n + 1)
                pool.tensor_tensor(w_lo[:, slot, :], w_st[:, slot, :], w_hi[:, slot, :].bitcast(F32),
                                   ALU.subtract).then_inc(w_ready, 1)

            pool.wait_ge(consts, 1)
            for p in range(2):
                for j in range(2):
                    n = BLOCKS * p + j
                    pool.wait_ge(w_in[j], 16 * (n // 2 + 1))
                    if p:
                        pool.wait_ge(unit_done, unit_no(0, BLOCKS + j - 1, 0) if j == 0 else unit_no(1, 0, 0))
                    split(j, n)
                with pool.Fori(1, BLOCKS // 2) as i:
                    for j in range(2):
                        pool.wait_ge(w_in[j], 16 * i + 16 * (BLOCKS * p // 2 + 1))
                        pool.wait_ge(unit_done, 2 * NT[p] * i + unit_no(p, j - 1, 0))
                        split(j, 2 * i + (BLOCKS * p + j))

        @block.tensor
        def _(pe):
            def half_unit(u, slot, hi, lo, c0, n, korder, half):
                ps = bank[u % 4][:, 0:n]
                for j in range(4 * half, 4 * half + 4):
                    kb = korder[j]
                    wh, wl = (w[:, slot, kb * P:(kb + 1) * P] for w in (w_hi, w_lo))
                    xh, xl = hi[:, kb, c0:c0 + n], lo[:, kb, c0:c0 + n]
                    pe.matmul(ps, wh, xh, start=(j == 0), stop=False)
                    pe.matmul(ps, wh, xl, start=False, stop=False)
                    mm = pe.matmul(ps, wl, xh, start=False, stop=(j == 7))
                if half:
                    mm.then_inc(unit_done, 1)

            def open_bank(a):
                if a >= 4:
                    drained(pe, a - 4)
                return aux[a % 4]

            def ones_sum(a, src, c0, n):
                pe.matmul(open_bank(a)[:, 0:n], ones[:, :], src[:, c0:c0 + n], start=True,
                          stop=True).then_inc(aux_done, 1)

            def final_sums(p):
                pe.wait_ge(f_sum, KB * sum(NT[:p + 1]))
                for t, (c0, w) in enumerate(TILES[p]):
                    ones_sum(AUX[(p, "NF", 0)] + t, rs, c0, w)

            def piece(p, name, i):
                a = AUX[(p, name, i)] if name != "NF" else None
                n = 4 * p + i
                if name == "RS":
                    pe.wait_ge(consts, 5)
                    pe.wait_ge(x_acc, KB * (p + 1))
                    for t, (c0, w) in enumerate(TILES[p]):
                        ones_sum(a + t, rs, c0, w)
                elif name == "NF":
                    final_sums(0)
                elif name == "VT":
                    for t in range(NT[p]):
                        evacuated(pe, unit_no(p, 5 * i + V, t))
                    for s, (c, m) in enumerate(chunk_sets(p)):
                        ps = open_bank(a + s)
                        for j in range(m):
                            lo_, hi_ = span(c + j)
                            mm = pe.transpose(ps[0:rows(c), j * P:(j + 1) * P], v[:, lo_:hi_], ident[:, :])
                        mm.then_inc(aux_done, 1)
                elif name == "D":
                    for t in range(NT[p]):
                        pe.wait_ge(post, post_no(p, 2, i, t) + 1)
                    for s, (c, m) in enumerate(chunk_sets(p)):
                        ps = open_bank(a + s)
                        for j in range(m):
                            lo_, hi_ = span(c + j)
                            mm = pe.matmul(ps[0:rows(c), j * P:j * P + rows(c)], k[:, lo_:hi_], q[:, lo_:hi_],
                                           start=True, stop=True)
                        mm.then_inc(aux_done, 1)
                elif name[0] == "L":
                    lv = int(name[1])
                    x = 1 << (lv - 1)
                    pe.wait_ge(level, 8 * n + lv)
                    ps = open_bank(a)
                    qv = q[:, 0:CH * NCH].rearrange("p (c n h x) -> p c n h x", c=NCH, h=2, x=x)
                    for c in range(NCH):
                        mm = pe.matmul(ps[:, 64 * c:64 * c + 64], k[:, CH * c:CH * c + CH], qv[:, c, :, 1, :],
                                       start=True, stop=True)
                    mm.then_inc(aux_done, 1)
                    if p and lv <= 4:
                        w = T8 if lv <= 2 else TAIL
                        q8 = q[:, CH * NCH:CH * NCH + w].rearrange("p (n h x) -> p n h x", h=2, x=x)
                        pe.matmul(open_bank(a + 1)[0:w, 0:w // 2], k[:, CH * NCH:CH * NCH + w], q8[:, :, 1, :],
                                  start=True, stop=True).then_inc(aux_done, 1)
                elif name == "KT":
                    pe.wait_ge(level, 8 * n + 8)
                    for s, (c, m) in enumerate(chunk_sets(p)):
                        ps = open_bank(a + s)
                        for j in range(m):
                            lo_, hi_ = span(c + j)
                            mm = pe.transpose(ps[0:rows(c), j * P:(j + 1) * P], k[:, lo_:hi_], ident[:, :])
                        mm.then_inc(aux_done, 1)
                elif name == "U":
                    for s in range(len(chunk_sets(p))):
                        drained(pe, AUX[(p, "VT", i)] + s)
                        drained(pe, AUX[(p, "KT", i)] + s)
                    for s, (c, m) in enumerate(chunk_sets(p)):
                        ps = open_bank(a + s)
                        for j in range(m):
                            r_ = CH if c < NCH else TAIL
                            mm = pe.matmul(ps[:, j * P:(j + 1) * P], k_tok[0:r_, c + j, :], v_tok[0:r_, c + j, :],
                                           start=True, stop=True)
                        mm.then_inc(aux_done, 1)
                    if p:
                        pe.wait_ge(s_step, s_at(p, i, "vm"))
                        for s in range(2):
                            pe.matmul(open_bank(a + 3 + s)[:, :], k_tok[0:T8, 8, :], tmp[0:T8, s, :],
                                      start=True, stop=True).then_inc(aux_done, 1)
                elif name == "O":
                    pe.wait_ge(s_step, s_at(p, i, "s7"))
                    if p:
                        drained(pe, AUX[(p, "U", i)] + 1)
                    for s, (c, m) in enumerate(chunk_sets(p)):
                        ps = open_bank(a + s)
                        for j in range(m):
                            lo_, hi_ = span(c + j)
                            out = ps[:, j * P:j * P + rows(c)]
                            if c < NCH:
                                pe.matmul(out, s_in[:, c + j, :], q[:, lo_:hi_], start=True, stop=False)
                                mm = pe.matmul(out, v_tok[:, c + j, :], attn[:, lo_:hi_], start=False, stop=True)
                                continue
                            pe.wait_ge(s_load, 16 * (i + 1))
                            pe.matmul(out, v_tok[0:T8, 8, :], attn[0:T8, lo_:hi_], start=True, stop=False,
                                      skip_group_check=True)
                            pe.matmul(ps[:, 0:TAIL], s_in[:, 8, :], q[:, lo_:lo_ + TAIL], start=False,
                                      stop=False, skip_group_check=True)
                            for b in range(NSEQ):
                                o_ = TAIL + SLEN * b
                                mm = pe.matmul(ps[:, o_:o_ + SLEN], s_smp[:, b, :],
                                               q[:, lo_ + o_:lo_ + o_ + SLEN], start=False,
                                               stop=(b == NSEQ - 1), skip_group_check=True)
                        mm.then_inc(aux_done, 1)
                elif name == "SS":
                    for s, (c, m) in enumerate(chunk_sets(p)):
                        drained(pe, AUX[(p, "O", i)] + s)
                        lo_, hi_ = span(c, m)
                        ones_sum(a + s, q, lo_, hi_ - lo_)
                elif name == "GATE":
                    pe.wait_ge(rg_step, rg_at(p, i, "sc3" if p else "c3"))
                    for t, (c0, w) in enumerate(TILES[p]):
                        for g, wt in enumerate((w_ra, w_rx)):
                            ps = open_bank(a + 2 * t + g)
                            pe.matmul(ps[:, 0:w], wt[:, i, :], xc[:, c0:c0 + w], start=True,
                                      stop=True).then_inc(aux_done, 1)

            def open_unit(u):
                if u >= 4:
                    evacuated(pe, u - 4)

            natural = list(range(KB))
            for p in range(2):
                nt = NT[p]
                for it, blk, t, half, pieces in schedule(p):
                    u = unit_no(p, blk, t)
                    c0, w = TILES[p][t]
                    if half == 0:
                        if t == 0:
                            pe.wait_ge(w_ready, BLOCKS * p + blk + 1)
                        open_unit(u)
                    if blk == 0 and t == 0:
                        if p == 0 and half == 0:
                            pe.wait_ge(const_in, 16 * 3)
                        pe.wait_ge(x_ready, KB * p + 4 * half + 4)
                    half_unit(u, blk % 2, a_hi, a_lo, c0, w, natural, half)
                    for name, i in pieces:
                        piece(p, name, i)
                for m in range(KB):
                    blk = OUT0 + m
                    pe.wait_ge(w_ready, BLOCKS * p + blk + 1)
                    for t, (c0, w) in enumerate(TILES[p]):
                        u = unit_no(p, blk, t)
                        open_unit(u)
                        for half in range(2):
                            if m == 0 and t == 0:
                                pe.wait_ge(y_ready, KB * p + 4 * half + 4)
                            half_unit(u, blk % 2, a_hi, a_lo, c0, w, OUT_ORDER, half)
                pe.wait_ge(b_sum, (KB - 1) * sum(NT[:p + 1]))
                for t, (c0, w) in enumerate(TILES[p]):
                    ones_sum(AUX[(p, "N2", 0)] + t, rs, c0, w)
                pe.wait_ge(b_lo_ready, KB * (nt + (NT[0] if p else 0)))
                hb = p * 8 * NT[0] * FF_GROUPS
                with pe.Fori(0, FF_GROUPS) as g:
                    for stage in range(2):
                        with pe.Fori(0, 2) as qd:
                            for j in range(4):
                                pe.wait_ge(w_ready, 16 * g + 4 * qd + (BLOCKS * p + MLP0 + 8 * stage + j + 1))
                                for t, (c0, w) in enumerate(TILES[p]):
                                    lu = j * nt + t
                                    pe.wait_ge(bank_free[lu % 4], 4 * nt * g + nt * qd
                                               + (unit_no(p, MLP0 + 8 * stage, 0) // 4 + lu // 4))
                                    if stage and j == 0:
                                        pe.wait_ge(h_ready, 8 * nt * g + (hb + 7 * nt + t + 1))
                                    hi, lo = (a_hi, a_lo) if stage else (b_hi, b_lo)
                                    for half in range(2):
                                        half_unit(lu, j % 2, hi, lo, c0, w, natural, half)
            final_sums(1)

        @block.scalar
        def _(act):
            def fn(out, in_, func, **kw):
                return nc.scalar.activation(out, in_, func, **kw)

            act.dma_start(par[:, :], par_d).then_inc(par_in, 16)

            def load_x(p, dst, b):
                x0 = TH[0] * p
                act.dma_start(dst[:, b, 0:TH[p]], xT[b, :, x0:x0 + TH[p]]).then_inc(x_in[b], 16)

            for b in range(2):
                load_x(0, xs, b)
            act.dma_start(ident[:, :], ident_d).then_inc(const_in, 16)
            for b in range(2, KB):
                load_x(0, xs, b)
            act.dma_start(w_ra[:, :, :], wra_d).then_inc(const_in, 16)
            act.dma_start(w_rx[:, :, :], wrx_d).then_inc(const_in, 16)

            def final_squares(p):
                evacuated(act, unit_no(p, BLOCKS - 1, NT[p] - 1))
                act.wait_ge(h_ready, 8 * FF_GROUPS * sum(NT[:p + 1]))
                for t, (c0, w) in enumerate(TILES[p]):
                    for b in range(KB):
                        if b >= 2 or t:
                            act.wait_ge(f_sum, KB * (NT[0] * p + t) + b - 1)
                        fn(tmp[:, b % 2, 0:w], xy[:, b, c0:c0 + w], ACT.Square).then_inc(f_sq, 1)

            def store(p):
                for b in range(KB):
                    act.wait_ge(y_out, KB * p + b + 1)
                    x0 = TH[0] * p
                    act.dma_start(y_d[b, :, x0:x0 + TH[p]], xy[:, b, 0:TH[p]]).then_inc(stored, 16)

            def load_small(p):
                act.dma_start(mask[:, :], mask_d).then_inc(smp_in, 16)
                if p == 0:
                    return
                act.dma_start(smask[:, :], smask_d).then_inc(smp_in, 16)
                act.dma_start(h0[:, :, :], h0_d).then_inc(smp_in, 16)
                act.dma_start(spad[:, :, :, 0:TAPS - 1], cs_d).then_inc(smp_in, 16)

            def load_state(i):
                act.dma_start(s_smp[:, :, :], ss_d[i]).then_inc(s_load, 16)

            def rsqrt_tiles(p, a):
                for t, (c0, w) in enumerate(TILES[p]):
                    filled(act, a + t)
                    fn(rs[:, c0:c0 + w], aux[(a + t) % 4][:, 0:w], ACT.Sqrt, bias=eps[:, 0:1],
                       scale=1.0 / DM).then_inc(aux_free[(a + t) % 4], 1)

            def piece(p, name, i):
                a = AUX[(p, name, i)]
                n = 4 * p + i
                if name == "RS":
                    act.wait_ge(consts, 5)
                    rsqrt_tiles(p, a)
                elif name in ("VT", "KT"):
                    dst = v_tok if name == "VT" else k_tok
                    if name == "VT" and i > 0:
                        filled(act, AUX[(p, "O", i - 1)] + 1 + p)
                    if name == "KT" and i > 0:
                        filled(act, AUX[(p, "U", i - 1)] + aux_uses(p, "U") - 1)
                    if name == "KT":
                        act.wait_ge(rg_step, rg_at(p, i, "scan"))
                    for s, (c, m) in enumerate(chunk_sets(p)):
                        filled(act, a + s)
                        fn(dst[0:rows(c), c:c + m, :],
                           aux[(a + s) % 4][0:rows(c), 0:m * P].rearrange("p (c d) -> p c d", d=P),
                           ACT.Copy).then_inc(aux_free[(a + s) % 4], 1)
                elif name == "O":
                    filled(act, a + len(chunk_sets(p)) - 1)
                    if p and i == 0:
                        act.wait_ge(stored, 16 * KB)
                    for s, (c, m) in enumerate(chunk_sets(p)):
                        lo_, hi_ = span(c, m)
                        ps = aux[(a + s) % 4][:, 0:hi_ - lo_]
                        fn(xy[:, i, lo_:hi_], ps, ACT.Copy)
                        fn(q[:, lo_:hi_], ps, ACT.Square).then_inc(aux_free[(a + s) % 4], 1)
                    if p and i + 1 < HEADS:
                        act.wait_ge(s_step, s_at(p, i, "smul"))
                        load_state(i + 1)
                    if p:
                        for s in (3, 4):
                            drained(act, AUX[(p, "U", i)] + s)
                        act.dma_start(ssn_d[i], tmp[:, :, :]).then_inc(s_store, 16)
                elif name == "SS":
                    for s, (c, m) in enumerate(chunk_sets(p)):
                        lo_, hi_ = span(c, m)
                        filled(act, a + s)
                        fn(k[:, lo_:hi_], aux[(a + s) % 4][:, 0:hi_ - lo_], ACT.Sqrt, bias=eps[:, 0:1],
                           scale=1.0 / P).then_inc(aux_free[(a + s) % 4], 1)
                elif name == "GATE":
                    if i > 0:
                        act.wait_ge(rg_step, rg_at(p, i - 1, "scan"))
                        filled(act, AUX[(p, "U", i - 1)] + aux_uses(p, "U") - 1)
                    for t, (c0, w) in enumerate(TILES[p]):
                        for g, (dst, b) in enumerate(((ta, "b_ra"), (ig, "b_rx"))):
                            u = a + 2 * t + g
                            filled(act, u)
                            fn(dst[:, c0:c0 + w], aux[u % 4][:, 0:w], ACT.Sigmoid,
                               bias=col(b, i)).then_inc(aux_free[u % 4], 1)
                    for t in range(NT[p]):
                        drained(act, a + 2 * t)
                    act.wait_ge(prep, PREP_STEPS)
                    fn(ea[:, 0:TH[p]], ta[:, 0:TH[p]], ACT.Exp, scale=sp[:, 3, i:i + 1])
                    fn(ta[:, 0:TH[p]], ta[:, 0:TH[p]], ACT.Tanh, scale=sp[:, 2, i:i + 1]).then_inc(rg_act, 1)
                    act.wait_ge(rg_step, rg_at(p, i, "v"))
                    fn(ea[:, 0:TH[p]], ea[:, 0:TH[p]], ACT.Sqrt, scale=-1.0).then_inc(rg_act, 1)

            def unit_fn(p, it, blk, t):
                u = unit_no(p, blk, t)
                c0, w = TILES[p][t]
                kind = blk - 5 * it if it < HEADS else None
                if kind in (G, Q):
                    pn = post_no(p, 0 if kind == G else 2, it, t)
                    evacuated(act, u)
                    if t >= 2:
                        act.wait_ge(post, pn - 1)
                    elif kind == Q:
                        act.wait_ge(post, post_no(p, 0, it, NT[p] - 1) + 1)
                        if p and it > 0:
                            act.wait_ge(s_store, 16 * it)
                    elif it > 0:
                        act.wait_ge(post, post_no(p, 2, it - 1, NT[p] - 1) + 1)
                    elif p:
                        act.wait_ge(f_sum, KB * NT[0])
                    src = gate[:, it % 2, c0:c0 + w] if kind == G else q[:, c0:c0 + w]
                    fn(tmp[:, t % 2, 0:w], src, ACT.Sigmoid).then_inc(act_fn, 1)
                elif kind == F:
                    evacuated(act, u)
                    if it > 0:
                        act.wait_ge(o_inv, O_STEPS * (4 * p + it - 1) + 2)
                    fn(k[:, c0:c0 + w], f[:, c0:c0 + w], ACT.Sigmoid, scale=-1.0)
                    fn(f[:, c0:c0 + w], f[:, c0:c0 + w], ACT.Sigmoid).then_inc(act_fn, 1)
                elif kind is None:
                    evacuated(act, u)
                    fn(ge[:, c0:c0 + w], ge[:, c0:c0 + w], ACT.Gelu_apprx_tanh).then_inc(act_fn, 1)

            act.wait_ge(par_in, 16)
            act.wait_ge(prep, 3)
            fn(sp[:, 0, :], sp[:, 0, :], ACT.Exp, scale=-1.0).then_inc(prep_act, 1)
            fn(lbv[:, 0, :], lbv[:, 0, :], ACT.Exp).then_inc(prep_act, 1)

            for p in range(2):
                th = TH[p]
                for b in range(KB):
                    act.wait_ge(x_in[b], 16 * (2 * p + 1))
                    if p and b == 0:
                        act.wait_ge(unit_done, unit_no(1, 0, 0))
                    fn(a_hi[:, b, 0:th], xs[:, b, 0:th], ACT.Copy, scale=col("ln_mix", b)).then_inc(x_hi, 1)
                if p:
                    final_squares(0)
                    rsqrt_tiles(0, AUX[(0, "NF", 0)])
                for b in range(KB):
                    if b >= 2:
                        act.wait_ge(x_acc, KB * p + b - 1)
                    fn(sq[b % 2][:, 0:th], xs[:, b, 0:th], ACT.Square).then_inc(x_sq, 1)
                if p:
                    store(0)
                act.wait_ge(x_acc, KB * p + KB)
                act.wait_ge(x_ready, KB * p + KB)
                load_small(p)
                if p:
                    load_state(0)
                for it, blk, t, half, pieces in schedule(p):
                    if ("RS", 0) in pieces:
                        piece(p, "RS", 0)
                    if half:
                        unit_fn(p, it, blk, t)
                    for name, i in pieces:
                        if name not in ("RS", "NF"):
                            piece(p, name, i)
                if p:
                    act.wait_ge(rg_step, rg_at(1, 3, "ncs"))
                    act.dma_start(hs_d, hout[:, :, :]).then_inc(small_out, 16)
                    act.dma_start(csn_d, ncs[:, :, :, :]).then_inc(small_out, 16)
                act.wait_ge(unit_done, unit_no(p, OUT0, 0))
                for n, b in enumerate(OUT_ORDER):
                    if b < HEADS:
                        act.wait_ge(o_inv, O_STEPS * (4 * p + b) + O_STEPS)
                    else:
                        act.wait_ge(post, post_no(p, 3, b - HEADS, NT[p] - 1) + 1)
                    fn(a_hi[:, b, 0:th], xy[:, b, 0:th], ACT.Copy).then_inc(y_hi, 1)
                for n, b in enumerate(OUT_ORDER):
                    act.wait_ge(y_ready, KB * p + n + 1)
                    load_x(p, xy, b)
                if p:
                    act.wait_ge(small_out, 16 * 2)
                    act.wait_ge(s_store, 16 * HEADS)
                for m in range(KB):
                    for t, (c0, w) in enumerate(TILES[p]):
                        u = unit_no(p, OUT0 + m, t)
                        bu = KB * NT[0] * p + m * NT[p] + t
                        evacuated(act, u)
                        fn(b_hi[:, m, c0:c0 + w], xy[:, m, c0:c0 + w], ACT.Copy, scale=col("ln_mlp", m))
                        if m == 0:
                            dst = rs[:, c0:c0 + w]
                        else:
                            dst = tmp[:, bu % 2, 0:w]
                            if m * NT[p] + t - 2 >= NT[p]:
                                act.wait_ge(b_sum, sum_no(p, m, t) - 2)
                        fn(dst, xy[:, m, c0:c0 + w], ACT.Square).then_inc(b_act, 1)
                rsqrt_tiles(p, AUX[(p, "N2", 0)])
                nt = NT[p]
                ub = unit_no(p, MLP0, 0) // 4
                with act.Fori(0, FF_GROUPS) as g:
                    with act.Fori(0, 2) as qd:
                        for j in range(4):
                            for t, (c0, w) in enumerate(TILES[p]):
                                lu = j * nt + t
                                act.wait_ge(bank_free[lu % 4], 4 * nt * g + nt * qd + (ub + lu // 4 + 1))
                                z = tmp[:, lu % 2, 0:w]
                                fn(a_hi[:, 4 * qd + j, c0:c0 + w], z, ACT.Square)
                                fn(z, z, ACT.Square).then_inc(h_sq, 1)
                if p == 0:
                    act.wait_ge(unit_done, unit_no(0, MLP0 + 16 * 3 + 8, 0))
                    for b in range(KB):
                        load_x(1, xs, b)
            final_squares(1)
            rsqrt_tiles(1, AUX[(1, "NF", 0)])
            store(1)
            act.wait_ge(rg_step, rg_at(1, 3, "ncs"))
            act.dma_start(hp_d, hprev[:, :]).then_inc(small_out, 16)
            act.dma_start(cp_d, xhist[:, :, :]).then_inc(small_out, 16)
            drained(act, AUX[(1, "U", 3)] + 2)
            act.dma_start(sp_d, state[:, :, :]).then_inc(small_out, 16)
            act.wait_ge(small_out, 16 * 5)
            act.wait_ge(s_store, 16 * HEADS)
            act.wait_ge(stored, 16 * KB * 2)

        @block.vector
        def _(dve):
            tt, ts, stt = dve.tensor_tensor, dve.tensor_scalar, dve.scalar_tensor_tensor
            count = {"prep": 0}

            def prep_step(ins):
                count["prep"] += 1
                ins.then_inc(prep, 1)
                dve.wait_ge(prep, count["prep"])

            def rg(p, i, name, ins):
                ins.then_inc(rg_step, 1)
                dve.wait_ge(rg_step, rg_at(p, i, name))

            def invert(p, which, a):
                for t, (c0, w) in enumerate(TILES[p]):
                    drained(dve, a + t)
                    dve.reciprocal(rs[:, c0:c0 + w], rs[:, c0:c0 + w]).then_inc(rs_ready, 1)
                dve.wait_ge(rs_ready, norms_before(p, which) + NT[p])

            def merge(p, head, lv):
                x = 1 << (lv - 1)
                n = TH[p] if lv <= 2 else (NP[p] if lv <= 4 else CH * NCH)
                qv, kv, fv = (b[:, 0:n].rearrange("p (n h x) -> p n h x", h=2, x=x) for b in (q, k, f))
                left, right = fv[:, :, 0, x - 1:x], fv[:, :, 1, x - 1:x]
                shape = [P, n // (2 * x), x]
                tt(qv[:, :, 1, :], qv[:, :, 1, :], left.broadcast_to(shape), ALU.mult)
                tt(kv[:, :, 0, :], kv[:, :, 0, :], right.broadcast_to(shape), ALU.mult).then_inc(spread, 1)
                dve.wait_ge(spread, LEVELS * head + lv)
                return tt(right, right, left, ALU.mult)

            def place(p, lv, a):
                if lv == 0:
                    for s, (c, m) in enumerate(chunk_sets(p)):
                        filled(dve, a + s)
                        r_ = rows(c)
                        lo_, hi_ = span(c, m)
                        mk = mask[0:r_, 0:r_].rearrange("p (o t) -> p o t", o=1).broadcast_to([r_, m, r_])
                        dve.copy_predicated(attn[0:r_, lo_:hi_].rearrange("p (c t) -> p c t", c=m), mk,
                                            aux[(a + s) % 4][0:r_, 0:m * r_].rearrange(
                                                "p (c t) -> p c t", c=m)).then_inc(aux_free[(a + s) % 4], 1)
                    return
                x = 1 << (lv - 1)
                m0 = P + 64 * (lv - 1)
                parts = [(a, P, 0, CH * NCH, NCH)]
                if p and lv <= 4:
                    w = T8 if lv <= 2 else TAIL
                    parts.append((a + 1, w, CH * NCH, CH * NCH + w, 1))
                for u, r_, lo_, hi_, nc_ in parts:
                    filled(dve, u)
                    w = (hi_ - lo_) // nc_ // 2
                    dst = attn[0:r_, lo_:hi_].rearrange("p (c n h x) -> p c n h x", c=nc_, h=2, x=x)[:, :, :, 1, :]
                    src = aux[u % 4][0:r_, 0:w * nc_].rearrange("p (c n x) -> p c n x", c=nc_, x=x)
                    mk = mask[0:r_, m0:m0 + w].rearrange("p (o n x) -> p o n x", o=1, x=x)
                    dve.copy_predicated(dst, mk.broadcast_to([r_, nc_, w // x, x]), src).then_inc(aux_free[u % 4], 1)

            def piece(p, name, i):
                a = AUX[(p, name, i)]
                n = 4 * p + i
                th = TH[p]
                if name == "RS":
                    invert(p, 0, a)
                elif name == "D":
                    if i > 0:
                        filled(dve, AUX[(p, "O", i - 1)] + 1 + p)
                    place(p, 0, a)
                    dve.wait_ge(post, post_no(p, 2, i, NT[p] - 1) + 1)
                    tt(q[:, 0:th], q[:, 0:th], f[:, 0:th], ALU.mult).then_inc(level, 1)
                elif name[0] == "L":
                    lv = int(name[1])
                    dve.wait_ge(level, 8 * n + lv)
                    place(p, lv, a)
                    merge(p, n, lv).then_inc(level, 1)
                elif name == "KT" and p:
                    drained(dve, AUX[(p, "VT", i)] + 2)
                    if i > 0:
                        dve.wait_ge(s_store, 16 * i)
                    dve.wait_ge(post, post_no(p, 0, min(i + 1, HEADS - 1), NT[p] - 1) + 1)
                    vm = tmp[0:T8, :, :].rearrange("p a (b d) -> p (a b) d", d=P)
                    tt(vm, v_tok[0:T8, 8:9, :].broadcast_to([T8, NSEQ, P]),
                       smask[0:T8, :].rearrange("p (b o) -> p b o", o=1).broadcast_to([T8, NSEQ, P]),
                       ALU.mult).then_inc(s_step, 1)
                elif name == "U":
                    dve.wait_ge(level, 8 * n + 8)
                    if i > 0:
                        filled(dve, AUX[(p, "O", i - 1)] + 1 + p)
                    dve.tensor_copy(s_in[:, 0, :], state[:, i, :]).then_inc(s_step, 1)
                    last = NCH + p
                    for c in range(last):
                        u = a + c // 4
                        filled(dve, u)
                        if c % 4 == 0 and c:
                            drained(dve, u - 1)
                        else:
                            dve.wait_ge(s_step, s_at(p, i, f"s{c}"))
                        end = CH * c + (CH if c < NCH else TAIL) - 1
                        dst = s_in[:, c + 1, :] if c + 1 < last else state[:, i, :]
                        ins = stt(dst, s_in[:, c, :], f[:, end:end + 1],
                                  aux[u % 4][:, (c % 4) * P:(c % 4 + 1) * P], ALU.mult, ALU.add)
                        if c % 4 == 3 or c == NCH:
                            ins.then_inc(aux_free[u % 4], 1)
                        else:
                            ins.then_inc(s_step, 1)
                    if p:
                        filled(dve, a + 4)
                        dve.wait_ge(s_load, 16 * (i + 1))
                        tot = f[:, NP[1] + SLEN - 1:TH[1]:SLEN].rearrange("p (b o) -> p b o", o=1)
                        new = tmp[:, :, :].rearrange("p a (b d) -> p (a b) d", d=P)
                        tt(new, s_smp[:, :, :], tot.broadcast_to([P, NSEQ, P]), ALU.mult).then_inc(s_step, 1)
                        dve.wait_ge(s_step, s_at(p, i, "smul"))
                        for s in range(2):
                            tt(tmp[:, s, :], tmp[:, s, :], aux[(a + 3 + s) % 4][:, :], ALU.add).then_inc(
                                aux_free[(a + 3 + s) % 4], 1)
                elif name == "SS":
                    o0 = O_STEPS * n
                    for s in range(len(chunk_sets(p))):
                        drained(dve, a + s)
                    dve.reciprocal(k[:, 0:th], k[:, 0:th]).then_inc(o_inv, 1)
                    dve.wait_ge(o_inv, o0 + 1)
                    y = xy[:, i, 0:th]
                    stt(y, y, col("gn"), k[:, 0:th], ALU.mult, ALU.mult).then_inc(o_inv, 1)
                    dve.wait_ge(o_inv, o0 + 2)
                    tt(y, y, gate[:, i % 2, 0:th], ALU.mult).then_inc(o_inv, 1)
                elif name == "GATE":
                    dve.wait_ge(rg_act, 2 * n + 1)
                    T, E, I = ta[:, 0:th], ea[:, 0:th], ig[:, 0:th]
                    rg(p, i, "u", stt(E, E, 1.0, T, ALU.add, ALU.mult))
                    rg(p, i, "a", ts(T, E, -1.0, 1.0, ALU.mult, ALU.add))
                    rg(p, i, "v", stt(E, E, 2.0, E, ALU.subtract, ALU.mult))
                    for t in range(NT[p]):
                        drained(dve, a + 2 * t + 1)
                    rg(p, i, "igx", tt(I, I, xc[:, 0:th], ALU.mult))
                    dve.wait_ge(rg_act, 2 * n + 2)
                    rg(p, i, "bt", tt(I, I, E, ALU.mult))
                    if p:
                        first = slice(NP[1], TH[1], SLEN)
                        rg(p, i, "fold", tt(fold[:, :], ta[:, first], h0[:, i, :], ALU.mult))
                        rg(p, i, "foldadd", tt(ig[:, first], ig[:, first], fold[:, :], ALU.add))
                        rg(p, i, "cut", dve.memset(ta[:, first], 0.0))
                    y = xy[:, HEADS + i, :]
                    if p and i == 0:
                        dve.wait_ge(stored, 16 * KB)
                    rg(p, i, "scan", dve.tensor_tensor_scan(y[:, 0:th], T, I, hprev[:, i:i + 1], ALU.mult, ALU.add))
                    rg(p, i, "hprev", dve.tensor_copy(hprev[:, i:i + 1], y[:, NP[p] - 1:NP[p]]))
                    rg(p, i, "xhist", dve.tensor_copy(xhist[:, i, :], xpad[:, NP[p]:NP[p] + TAPS - 1]))
                    if p:
                        rg(p, i, "hout", dve.tensor_copy(hout[:, i, :], y[:, NP[1] + SLEN - 1:TH[1]:SLEN]))
                        rg(p, i, "ncs", dve.tensor_copy(ncs[:, i, :, :], spad[:, i, :, SLEN:SLEN + TAPS - 1]))

            def read_out(p, it, blk, t):
                u = unit_no(p, blk, t)
                c0, w = TILES[p][t]
                kind = blk - 5 * it if it < HEADS else None
                ps = bank[u % 4]
                if kind == V and it > 0:
                    filled(dve, AUX[(p, "VT", it - 1)] + 1 + p)
                if kind == Q and it > 0:
                    filled(dve, AUX[(p, "SS", it - 1)] + 1 + p)
                if kind is None and blk > GA0:
                    dve.wait_ge(post, post_no(p, 3, blk - GA0 - 1, t) + 1)
                dve.wait_ge(unit_done, u + 1)
                if kind == XA and c0 + w > NP[p]:
                    n = NP[p] - c0
                    tt(xpad[:, TAPS - 1 + c0:TAPS - 1 + NP[p]], ps[:, 0:n], rs[:, c0:c0 + n], ALU.mult)
                    tt(spad[:, it, :, TAPS - 1:], ps[:, n:w].rearrange("p (b s) -> p b s", s=SLEN),
                       rs[:, NP[p]:c0 + w].rearrange("p (b s) -> p b s", s=SLEN),
                       ALU.mult).then_inc(bank_free[u % 4], 1)
                    return
                dst = {V: v[:, c0:c0 + w], G: gate[:, it % 2, c0:c0 + w], F: f[:, c0:c0 + w], Q: q[:, c0:c0 + w],
                       XA: xpad[:, TAPS - 1 + c0:min(TAPS - 1 + c0 + w, TAPS - 1 + NP[p])], None: ge[:, c0:c0 + w]}[kind]
                tt(dst, ps[:, 0:w], rs[:, c0:c0 + w], ALU.mult).then_inc(bank_free[u % 4], 1)

            def finish_unit(p, it, blk, t):
                c0, w = TILES[p][t]
                kind = blk - 5 * it if it < HEADS else None
                if kind in (V, XA):
                    return
                pn = post_no(p, {G: 0, F: 1, Q: 2, None: 3}[kind], it if it < HEADS else blk - GA0, t)
                dve.wait_ge(act_fn, pn + 1)
                z = tmp[:, t % 2, 0:w]
                if kind == G:
                    d = gate[:, it % 2, c0:c0 + w]
                    tt(d, d, z, ALU.mult).then_inc(post, 1)
                elif kind == Q:
                    stt(q[:, c0:c0 + w], q[:, c0:c0 + w], QSCALE, z, ALU.mult, ALU.mult).then_inc(post, 1)
                elif kind == F:
                    fc, kc = f[:, c0:c0 + w], k[:, c0:c0 + w]
                    if p == 0 and it == 0 and t == 0:
                        dve.wait_ge(prep, PREP_STEPS)
                    ts(fc, fc, lbv[:, 1, it:it + 1], lbv[:, 0, it:it + 1], ALU.mult, ALU.add).then_inc(post_half, 1)
                    ts(kc, kc, lbv[:, 1, it:it + 1], None, ALU.mult)
                    dve.wait_ge(post_half, (p * 4 * NT[0]) + it * NT[p] + t + 1)
                    ts(fc, fc, F_MIN, None, ALU.max).then_inc(post, 1)
                else:
                    c = blk - GA0
                    y = xy[:, HEADS + c, c0:c0 + w]
                    tt(y, y, ge[:, c0:c0 + w], ALU.mult).then_inc(post, 1)

            def convolve(p, i):
                for t in range(NT[p]):
                    evacuated(dve, unit_no(p, 5 * i + XA, t))
                rg(p, i, "hist", dve.tensor_copy(xpad[:, 0:TAPS - 1], xhist[:, i, :]))

                def taps(out, src, names):
                    for j, name in enumerate(names):
                        wj = col("conv_w", 4 * i + j)
                        if j == 0:
                            rg(p, i, name, ts(out, src(0), wj, col("conv_b", i), ALU.mult, ALU.add))
                        else:
                            rg(p, i, name, stt(out, src(j), wj, out, ALU.mult, ALU.add))

                taps(xc[:, 0:NP[p]], lambda j: xpad[:, j:j + NP[p]], ["c0", "c1", "c2", "c3"])
                if p:
                    taps(xc[:, NP[1]:TH[1]].rearrange("p (b s) -> p b s", s=SLEN),
                         lambda j: spad[:, i, :, j:j + SLEN], ["sc0", "sc1", "sc2", "sc3"])

            def final_dve(p):
                for t, (c0, w) in enumerate(TILES[p]):
                    for b in range(KB):
                        n = KB * (NT[0] * p + t) + b
                        dve.wait_ge(f_sq, n + 1)
                        r_, z = rs[:, c0:c0 + w], tmp[:, b % 2, 0:w]
                        if b == 0:
                            ins = dve.tensor_copy(r_, z)
                        else:
                            dve.wait_ge(f_sum, n)
                            ins = tt(r_, r_, z, ALU.add)
                        ins.then_inc(f_sum, 1)
                invert(p, 2, AUX[(p, "NF", 0)])
                for b in range(KB):
                    y = xy[:, b, 0:TH[p]]
                    stt(y, y, col("ln_final", b), rs[:, 0:TH[p]], ALU.mult, ALU.mult).then_inc(y_out, 1)

            lam = par[:, PC["lam"]:PC["lam"] + 4]
            lb_in = par[:, PC["lb"]:PC["lb"] + 4]
            dve.wait_ge(par_in, 16)
            prep_step(ts(sp[:, 1, :], lam, -1.0, None, ALU.mult))
            prep_step(tt(sp[:, 0, :], sp[:, 1, :], lam, ALU.max))
            prep_step(tt(lbv[:, 0, :], lb_in, lb_in, ALU.subtract))
            dve.wait_ge(prep_act, 2)
            prep_step(dve.reciprocal(lbv[:, 1, :], lbv[:, 0, :]))
            prep_step(tt(lbv[:, 0, :], lbv[:, 0, :], lbv[:, 1, :], ALU.mult))
            prep_step(tt(lbv[:, 0, :], lbv[:, 0, :], lbv[:, 0, :], ALU.subtract))
            prep_step(ts(lbv[:, 0, :], lbv[:, 0, :], 0.0, 1.0, ALU.max, ALU.min))
            prep_step(ts(lbv[:, 1, :], lbv[:, 0, :], -1.0, 1.0, ALU.mult, ALU.add))
            prep_step(ts(sp[:, 2, :], sp[:, 0, :], 2.0, None, ALU.add))
            prep_step(dve.reciprocal(sp[:, 2, :], sp[:, 2, :]))
            prep_step(tt(sp[:, 0, :], sp[:, 0, :], sp[:, 2, :], ALU.mult))
            prep_step(tt(sp[:, 2, :], sp[:, 0, :], sp[:, 0, :], ALU.mult))
            prep_step(ts(sp[:, 3, :], sp[:, 2, :], 1.0 / 17, None, ALU.mult))
            for d in (15, 13, 11, 9, 7, 5, 3):
                prep_step(stt(sp[:, 3, :], sp[:, 3, :], 1.0 / d, sp[:, 2, :], ALU.add, ALU.mult))
            prep_step(stt(sp[:, 3, :], sp[:, 3, :], 1.0, sp[:, 0, :], ALU.add, ALU.mult))
            prep_step(ts(sp[:, 3, :], sp[:, 3, :], 2.0, None, ALU.mult))
            prep_step(stt(sp[:, 1, :], sp[:, 1, :], 0.0, sp[:, 3, :], ALU.max, ALU.add))
            prep_step(ts(sp[:, 2, :], sp[:, 1, :], 4.0, None, ALU.mult))
            prep_step(ts(sp[:, 3, :], sp[:, 1, :], -8.0, None, ALU.mult))
            assert count["prep"] == PREP_STEPS

            for p in range(2):
                th, nt = TH[p], NT[p]
                for b in range(KB):
                    dve.wait_ge(x_hi, KB * p + b + 1)
                    stt(a_lo[:, b, 0:th], xs[:, b, 0:th], col("ln_mix", b), a_hi[:, b, 0:th].bitcast(F32),
                        ALU.mult, ALU.subtract).then_inc(x_ready, 1)
                if p:
                    final_dve(0)
                    dve.wait_ge(y_out, KB)
                for b in range(KB):
                    dve.wait_ge(x_sq, KB * p + b + 1)
                    if b == 0:
                        ins = dve.tensor_copy(rs[:, 0:th], sq[0][:, 0:th])
                    else:
                        dve.wait_ge(x_acc, KB * p + b)
                        ins = tt(rs[:, 0:th], rs[:, 0:th], sq[b % 2][:, 0:th], ALU.add)
                    ins.then_inc(x_acc, 1)
                dve.memset(attn[:, :], 0.0).then_inc(zeroed, 1)
                dve.wait_ge(zeroed, p + 1)
                dve.wait_ge(smp_in, 16 * (1 + 4 * p))
                dve.wait_ge(consts, 5)
                pending = []
                queue = []
                started = False
                for it, blk, t, half, pieces in schedule(p):
                    names = [n_ for n_, _ in pieces]
                    if "RS" in names:
                        piece(p, "RS", 0)
                        started = True
                    if half:
                        queue.append((it, blk, t))
                    while started and queue:
                        un = queue.pop(0)
                        read_out(p, *un)
                        if un[1] == 5 * un[0] + XA and un[0] < HEADS and un[2] == nt - 1:
                            convolve(p, un[0])
                        pending.append(un)
                        if len(pending) > 1:
                            finish_unit(p, *pending.pop(0))
                    last_of_iteration = half and t == nt - 1 and blk in (5 * it + Q, GA0 + 3)
                    if last_of_iteration:
                        while pending:
                            finish_unit(p, *pending.pop(0))
                    for name, i in pieces:
                        if name not in ("RS", "NF"):
                            piece(p, name, i)
                for n, b in enumerate(OUT_ORDER):
                    dve.wait_ge(y_hi, KB * p + n + 1)
                    tt(a_lo[:, b, 0:th], xy[:, b, 0:th], a_hi[:, b, 0:th].bitcast(F32),
                       ALU.subtract).then_inc(y_ready, 1)
                for m in range(KB):
                    dve.wait_ge(x_in[m], 16 * (2 * p + 2))
                    for t, (c0, w) in enumerate(TILES[p]):
                        u = unit_no(p, OUT0 + m, t)
                        bu = KB * NT[0] * p + m * nt + t
                        x = xy[:, m, c0:c0 + w]
                        dve.wait_ge(unit_done, u + 1)
                        tt(x, x, bank[u % 4][:, 0:w], ALU.add).then_inc(bank_free[u % 4], 1)
                        dve.wait_ge(b_act, bu + 1)
                        stt(b_lo[:, m, c0:c0 + w], x, col("ln_mlp", m), b_hi[:, m, c0:c0 + w].bitcast(F32),
                            ALU.mult, ALU.subtract).then_inc(b_lo_ready, 1)
                        if m:
                            if m > 1:
                                dve.wait_ge(b_sum, sum_no(p, m - 1, t))
                            r_ = rs[:, c0:c0 + w]
                            tt(r_, r_, tmp[:, bu % 2, 0:w], ALU.add).then_inc(b_sum, 1)
                invert(p, 1, AUX[(p, "N2", 0)])
                ub = unit_no(p, MLP0, 0)
                hb = p * 8 * NT[0] * FF_GROUPS
                with dve.Fori(0, FF_GROUPS) as g:
                    with dve.Fori(0, 2) as qd:
                        for j in range(4):
                            for t, (c0, w) in enumerate(TILES[p]):
                                lu = j * nt + t
                                dve.wait_ge(unit_done, 16 * nt * g + 4 * nt * qd + (ub + lu + 1))
                                z = tmp[:, lu % 2, 0:w]
                                stt(z, bank[lu % 4][:, 0:w], 0.0, rs[:, c0:c0 + w], ALU.max,
                                    ALU.mult).then_inc(bank_free[lu % 4], 1)
                                dve.wait_ge(h_sq, 8 * nt * g + 4 * nt * qd + (hb + lu + 1))
                                tt(a_lo[:, 4 * qd + j, c0:c0 + w], z, a_hi[:, 4 * qd + j, c0:c0 + w].bitcast(F32),
                                   ALU.subtract).then_inc(h_ready, 1)
                    with dve.Fori(0, 2) as qd:
                        for j in range(4):
                            for t, (c0, w) in enumerate(TILES[p]):
                                lu = j * nt + t
                                dve.wait_ge(unit_done, 16 * nt * g + 4 * nt * qd + (ub + 8 * nt + lu + 1))
                                x = xy[:, 4 * qd + j, c0:c0 + w]
                                tt(x, x, bank[lu % 4][:, 0:w], ALU.add).then_inc(bank_free[lu % 4], 1)
            final_dve(1)


def _weight_blocks(w_in, w_out, w_up, w_down):
    def blk(w, r0, c0):
        return w[r0:r0 + DM, c0:c0 + P].reshape(KB, P, P).transpose(1, 0, 2).reshape(P, DM)

    half = DM // 2
    xa0, ga0, q0, f0, v0, g0 = (half * j for j in range(6))
    out = []
    for i in range(HEADS):
        out += [blk(w_in, 0, c + P * i) for c in (v0, g0, xa0, f0, q0)]
    out += [blk(w_in, 0, ga0 + P * c) for c in range(4)]
    w_o = np.concatenate([w_out[half:], w_out[:half]], axis=0)
    out += [blk(w_o, 0, P * m) for m in range(KB)]
    for g in range(FF_GROUPS):
        out += [blk(w_up, 0, DM * g + P * m) for m in range(KB)]
        out += [blk(w_down, DM * g, P * m) for m in range(KB)]
    return np.stack(out)


def _masks():
    s = np.arange(P)[:, None]
    out = [(s == np.arange(P)[None, :])]
    j = np.arange(64)[None, :]
    for lv in range(1, LEVELS + 1):
        x = 1 << (lv - 1)
        t = (j // x) * 2 * x + x + j % x
        out.append((s // (2 * x) == t // (2 * x)) & (s % (2 * x) < x))
    return np.concatenate(out, axis=1).astype(np.int32)


def kernel(x_prompt, x_sample, state_rglru_h, state_rglru_conv, state_hgrn2, meta_tokens, ln_mix, w_in, conv_w,
           conv_b, w_rg_a, b_rg_a, w_rg_x, b_rg_x, rg_lambda, hgrn_lb, hgrn_norm, w_out, ln_mlp, w_up, w_down,
           ln_final):
    import concourse.bacc as bacc
    from concourse.bass_utils import run_bass_kernel_spmd

    A = np.asarray
    x = np.concatenate([A(meta_tokens), A(x_prompt)[0], A(x_sample).reshape(NSMP, DM)], axis=0)
    cols = lambda a, n: A(a).reshape(n, P).T

    def diagonal(w):
        w = A(w)[0]
        out = np.zeros((P, 4, P), w.dtype)
        for h in range(8):
            r0 = 64 * (h % 2)
            out[r0:r0 + 64, h // 2, r0:r0 + 64] = w[h]
        return out

    taps = A(conv_w)[0].reshape(TAPS, 4, P).transpose(2, 1, 0).reshape(P, 16)
    params = np.concatenate([cols(ln_mix, 8), cols(ln_mlp, 8), cols(ln_final, 8), taps, cols(conv_b, 4),
                             cols(b_rg_a, 4), cols(b_rg_x, 4), cols(rg_lambda, 4), cols(hgrn_lb, 4),
                             A(hgrn_norm).reshape(P, 1)], axis=1)
    smask = np.zeros((T8, NSEQ), np.float32)
    for b in range(NSEQ):
        smask[TAIL + SLEN * b:TAIL + SLEN * (b + 1), b] = 1.0
    arrays = {
        "xT": x.T.reshape(KB, P, x.shape[0]),
        "wall": _weight_blocks(A(w_in)[0], A(w_out)[0], A(w_up)[0], A(w_down)[0]),
        "params": params,
        "w_ra": diagonal(w_rg_a),
        "w_rx": diagonal(w_rg_x),
        "h0": A(state_rglru_h)[0].reshape(NSEQ, 4, P).transpose(2, 1, 0),
        "conv0": A(state_rglru_conv)[0].reshape(NSEQ, TAPS - 1, 4, P).transpose(3, 2, 0, 1),
        "state0": A(state_hgrn2)[0].transpose(1, 2, 0, 3),
        "ident": np.eye(P, dtype=np.float32),
        "mask": _masks(),
        "smask": smask,
    }
    outs = {"y": (KB, P, x.shape[0]), "hp": (P, 4), "cp": (P, 4, TAPS - 1), "sp_out": (P, HEADS, P),
            "hs": (P, 4, NSEQ), "csn": (P, 4, NSEQ, TAPS - 1), "ssn": (HEADS, P, NSEQ, P)}

    nc = bacc.Bacc("TRN2", target_bir_lowering=False, num_devices=1)
    arrays = {n: np.ascontiguousarray(a) for n, a in arrays.items()}
    ins = [nc.dram_tensor(f"in_{n}", a.shape, mybir.dt.from_np(a.dtype), kind="ExternalInput").ap()
           for n, a in arrays.items()]
    outputs = [nc.dram_tensor(f"out_{n}", s, F32, kind="ExternalOutput").ap() for n, s in outs.items()]
    build(nc, ins, outputs)
    r = run_bass_kernel_spmd(nc, [{f"in_{n}": a for n, a in arrays.items()}], core_ids=[0])
    y, hp, cp, sp, hs, csn, ssn = (r.results[0][f"out_{n}"] for n in outs)

    yt = y.reshape(DM, -1).T
    return (yt[META:META + SEQ].reshape(1, SEQ, DM),
            yt[META + SEQ:].reshape(NSEQ, SLEN, DM),
            hp.T.reshape(1, 1, DM // 2),
            cp.transpose(2, 1, 0).reshape(1, 1, TAPS - 1, DM // 2),
            sp.transpose(1, 0, 2).reshape(1, 1, HEADS, P, P),
            hs.transpose(2, 1, 0).reshape(1, NSEQ, DM // 2),
            csn.transpose(2, 3, 1, 0).reshape(1, NSEQ, TAPS - 1, DM // 2),
            ssn.transpose(2, 0, 1, 3).reshape(1, NSEQ, HEADS, P, P))
```

```python
from contextlib import ExitStack

import numpy as np

import concourse.bass as bass
from concourse import mybir

F32 = mybir.dt.float32
F32R = mybir.dt.float32r
I32 = mybir.dt.int32
ALU = mybir.AluOpType
ACT = mybir.ActivationFunctionType

P = 128
DM = 1024
KB = DM // P
META, SEQ = 16, 2048
NSEQ, SLEN = 8, 4
NSMP = NSEQ * SLEN
HEADS = 4
CH = 128
LEVELS = 7
TAPS = 4
FF_GROUPS = 4
EPS = 1e-6
F_MIN = 1e-30
QSCALE = float(P) ** -0.5

TH = [1024, META + SEQ - 1024 + NSMP]
NP = [1024, META + SEQ - 1024]
TAIL = NP[1] - 1024
T8 = TAIL + NSMP
TMAX = TH[1]
TILES = [[(0, 512), (512, 512)], [(0, 358), (358, 358), (716, 356)]]
NT = [2, 3]
NCH = 8
BLOCKS = 96
V, G, XA, F, Q = range(5)
GA0, OUT0, MLP0 = 20, 24, 32
OUT_ORDER = [0, 1, 2, 4, 5, 6, 7, 3]

PC = {}
_at = 0
for _name, _n in (("ln_mix", 8), ("ln_mlp", 8), ("ln_final", 8), ("conv_w", 16), ("conv_b", 4), ("b_ra", 4),
                  ("b_rx", 4), ("lam", 4), ("lb", 4), ("gn", 1)):
    PC[_name] = _at
    _at += _n
NPARAM = _at


def unit_no(p, blk, t):
    return p * BLOCKS * NT[0] + blk * NT[p] + t


def tile_no(p, t, b):
    return KB * (NT[0] * p + t) + b + 1


def final_no(p, m, t):
    return KB * NT[0] * p + m * NT[p] + t + 1


def sum_no(p, m, t):
    return (KB - 1) * NT[0] * p + (m - 1) * NT[p] + t + 1


def post_no(p, kind, i, t):
    base = p * 16 * NT[0]
    return base + (i * 3 + kind) * NT[p] + t if kind < 3 else base + (12 + i) * NT[p] + t


RG_STEPS = [
    ["hist", "c0", "c1", "c2", "c3", "u", "a", "v", "igx", "bt", "scan", "hprev", "xhist"],
    ["hist", "c0", "c1", "c2", "c3", "sc0", "sc1", "sc2", "sc3", "u", "a", "v", "igx", "bt", "fold", "foldadd",
     "cut", "scan", "hprev", "xhist", "hout", "ncs"],
]


def rg_at(p, i, name):
    return p * 4 * len(RG_STEPS[0]) + i * len(RG_STEPS[p]) + RG_STEPS[p].index(name) + 1


S_STEPS = [["s0", "s1", "s2", "s3", "s5", "s6", "s7"],
           ["vm", "s0", "s1", "s2", "s3", "s5", "s6", "s7", "smul"]]


def s_at(p, i, name):
    return p * 4 * len(S_STEPS[0]) + i * len(S_STEPS[p]) + S_STEPS[p].index(name) + 1


O_STEPS = 4
PREP_STEPS = 25
PIECES = ["VT", "D"] + [f"L{l}" for l in range(1, 8)] + ["KT", "U", "O", "SS", "S1", "S2", "S3"]
SLOTS = [dict(zip(range(16), PIECES)),
         dict(zip([0, 4, 5, 6, 8, 9, 10, 12, 13, 14, 15, 16, 18, 19, 21, 22], PIECES))]
GATE_SLOT = [16, 24]
SQUARES_AFTER = {1: [0], 2: [1], 3: [2], 4: [3], 5: [4, 5], 6: [6, 7]}
RS_SLOT = [7, 1]
FINAL_SLOTS = {3: ("NF", 0), 4: ("FN", 0), 5: ("FN", 1), **{8 + b: ("FY", b) for b in range(8)}}


def schedule(p):
    out = []
    for i in range(HEADS + 1):
        blks = [5 * i + b for b in range(5)] if i < HEADS else [GA0 + c for c in range(4)]
        s = 0
        for blk in blks:
            for t in range(NT[p]):
                for half in range(2):
                    pieces = []
                    if p and i == 0 and s in FINAL_SLOTS:
                        pieces.append(FINAL_SLOTS[s])
                    if i == 0 and s == RS_SLOT[p]:
                        pieces.append(("RS", 0))
                    if i >= 1 and s in SLOTS[p]:
                        pieces.append((SLOTS[p][s], i - 1))
                    if i < HEADS and s == GATE_SLOT[p]:
                        pieces.append(("GATE", i))
                    out.append((i, blk, t, half, pieces))
                    s += 1
    return out


def aux_uses(p, name):
    if name in ("FN", "FY", "S1", "S2", "S3"):
        return 0
    if name in ("RS", "N2", "NF"):
        return NT[p]
    if name == "GATE":
        return 2 * NT[p]
    if name[0] == "L":
        return 1 + (p == 1 and int(name[1]) <= 4)
    if name == "U":
        return 2 + 3 * p
    return 2 + p


def number_aux():
    at, n, seen = {}, 0, []
    for p in range(2):
        order = [(name, i) for *_, pieces in schedule(p) for name, i in pieces] + [("N2", 0)] + [("NF", 0)] * p
        for name, i in order:
            own = p
            if name == "NF":
                own = len(seen)
                seen.append(name)
            at[(own, name, i)] = n
            n += aux_uses(own, name)
    return at


AUX = number_aux()


def build(nc, ins, outs):
    (xT, wall, par_d, wra_d, wrx_d, h0_d, cs_d, ss_d, ident_d, mask_d, smask_d) = ins
    (y_d, hp_d, cp_d, sp_d, hs_d, csn_d, ssn_d) = outs

    with ExitStack() as ctx:
        def sb(name, shape, dt=F32, stack=ctx):
            return stack.enter_context(nc.sbuf_tensor(name, shape, dt))

        def sem(name):
            return ctx.enter_context(nc.semaphore(name))

        a_hi = sb("a_hi", [P, KB, TMAX], F32R)
        a_lo = sb("a_lo", [P, KB, TMAX], F32R)
        xy = sb("xy", [P, KB, TMAX])
        w_st = sb("w_st", [P, 2, DM])
        w_hi = sb("w_hi", [P, 2, DM], F32R)
        w_lo = sb("w_lo", [P, 2, DM], F32R)
        rs = sb("rs", [P, TMAX])
        tmp = sb("tmp", [P, 2, 512])
        state = sb("state", [P, HEADS, P])
        ident = sb("ident", [P, P])
        ones = sb("ones", [P, P])
        par = sb("par", [P, NPARAM])
        eps = sb("eps", [P, 1])
        sp = sb("sp", [P, 4, 4])
        lbv = sb("lbv", [P, 2, 4])
        hprev = sb("hprev", [P, 4])
        xhist = sb("xhist", [P, 4, TAPS - 1])
        w_ra = sb("w_ra", [P, 4, P])
        w_rx = sb("w_rx", [P, 4, P])
        with ExitStack() as r:
            q = sb("q", [P, TMAX], stack=r)
            k = sb("k", [P, TMAX], stack=r)
            f = sb("f", [P, TMAX], stack=r)
            v = sb("v", [P, TMAX], stack=r)
            gate = sb("gate", [P, 2, TMAX], stack=r)
            with ExitStack() as r2:
                xs = sb("xs", [P, KB, TMAX], stack=r2)
            v_tok = sb("v_tok", [P, 9, P], stack=r)
            k_tok = sb("k_tok", [P, 9, P], stack=r)
            attn = sb("attn", [P, TMAX], stack=r)
            s_in = sb("s_in", [P, 9, P], stack=r)
            s_smp = sb("s_smp", [P, NSEQ, P], stack=r)
            xpad = sb("xpad", [P, TAPS - 1 + NP[1]], stack=r)
            xc = sb("xc", [P, TMAX], stack=r)
            ta = sb("ta", [P, TMAX], stack=r)
            ea = sb("ea", [P, TMAX], stack=r)
            spad = sb("spad", [P, 4, NSEQ, TAPS - 1 + SLEN], stack=r)
            h0 = sb("h0", [P, 4, NSEQ], stack=r)
            hout = sb("hout", [P, 4, NSEQ], stack=r)
            ncs = sb("ncs", [P, 4, NSEQ, TAPS - 1], stack=r)
            fold = sb("fold", [P, NSEQ], stack=r)
            mask = sb("mask", [P, P + LEVELS * 64], I32, stack=r)
            smask = sb("smask", [T8, NSEQ], stack=r)
        b_hi = sb("b_hi", [P, KB, TMAX], F32R)
        b_lo = sb("b_lo", [P, KB, TMAX], F32R)
        ig = k_tok[:, :, :].rearrange("p c d -> p (c d)")
        ge = xc
        sq = [q, k]
        rf = gate[:, 1, :]

        bank = [ctx.enter_context(nc.psum_tensor(f"bank{j}", [P, 512], F32)) for j in range(4)]
        aux = [ctx.enter_context(nc.psum_tensor(f"aux{j}", [P, 512], F32)) for j in range(4)]

        w_in = [sem("w_in0"), sem("w_in1")]
        w_split = sem("w_split")
        w_ready = sem("w_ready")
        unit_done = sem("unit_done")
        bank_free = [sem(f"bank_free{j}") for j in range(4)]
        aux_done = sem("aux_done")
        aux_free = [sem(f"aux_free{j}") for j in range(4)]
        const_in = sem("const_in")
        par_in = sem("par_in")
        smp_in = sem("smp_in")
        consts = sem("consts")
        prep_act = sem("prep_act")
        prep = sem("prep")
        x_in = [sem(f"x_in{b}") for b in range(KB)]
        x_in2 = [sem(f"x_in2_{b}") for b in range(KB)]
        x_hi = sem("x_hi")
        x_ready = sem("x_ready")
        x_sq = sem("x_sq")
        x_acc = sem("x_acc")
        rs_ready = sem("rs_ready")
        rf_ready = sem("rf_ready")
        act_fn = sem("act_fn")
        post = sem("post")
        post_half = sem("post_half")
        zeroed = sem("zeroed")
        spread = sem("spread")
        level = sem("level")
        s_step = sem("s_step")
        s_load = sem("s_load")
        s_store = sem("s_store")
        rg_step = sem("rg_step")
        rg_act = sem("rg_act")
        o_inv = sem("o_inv")
        y_hi = sem("y_hi")
        y_ready = sem("y_ready")
        b_act = sem("b_act")
        b_lo_ready = sem("b_lo_ready")
        b_sum = sem("b_sum")
        h_sq = sem("h_sq")
        h_ready = sem("h_ready")
        f_sq = sem("f_sq")
        f_sum = sem("f_sum")
        y_out = sem("y_out")
        stored = sem("stored")
        small_out = sem("small_out")

        def evacuated(eng, u):
            eng.wait_ge(bank_free[u % 4], u // 4 + 1)

        def filled(eng, a):
            eng.wait_ge(aux_done, a + 1)

        def drained(eng, a):
            eng.wait_ge(aux_free[a % 4], a // 4 + 1)

        def col(name, j=0):
            return par[:, PC[name] + j:PC[name] + j + 1]

        def norms_before(p, which):
            return 2 * NT[0] * p + which * NT[p]

        def chunk_sets(p):
            return [(0, 4), (4, 4)] + ([(8, 1)] if p else [])

        def span(c, n=1):
            return (CH * c, CH * c + (CH * n if c < NCH else T8))

        def rows(c):
            return CH if c < NCH else T8

        block = ctx.enter_context(nc.Block())

        @block.sync
        def _(sync):
            def load(p, m, slot):
                sync.dma_start(w_st[:, slot, :], wall[m]).then_inc(w_in[slot], 16)

            for p in range(2):
                for j in range(2):
                    if p:
                        sync.wait_ge(w_ready, BLOCKS * p + j - 1)
                    load(p, j, j)
                with sync.Fori(1, BLOCKS // 2) as i:
                    for j in range(2):
                        sync.wait_ge(w_ready, 2 * i + (BLOCKS * p + j - 1))
                        load(p, 2 * i + j, j)

        @block.gpsimd
        def _(pool):
            pool.memset(ones[:, :], 1.0).then_inc(consts, 1)
            pool.memset(eps[:, :], EPS).then_inc(consts, 1)
            pool.memset(hprev[:, :], 0.0).then_inc(consts, 1)
            pool.memset(xhist[:, :, :], 0.0).then_inc(consts, 1)
            pool.memset(state[:, :, :], 0.0).then_inc(consts, 1)

            def split(slot, n):
                pool.tensor_tensor(w_hi[:, slot, :], w_st[:, slot, :], ones[:, 0:1].broadcast_to([P, DM]),
                                   ALU.mult).then_inc(w_split, 1)
                pool.wait_ge(w_split, n + 1)
                pool.tensor_tensor(w_lo[:, slot, :], w_st[:, slot, :], w_hi[:, slot, :].bitcast(F32),
                                   ALU.subtract).then_inc(w_ready, 1)

            pool.wait_ge(consts, 1)
            for p in range(2):
                for j in range(2):
                    n = BLOCKS * p + j
                    pool.wait_ge(w_in[j], 16 * (n // 2 + 1))
                    if p:
                        pool.wait_ge(unit_done, unit_no(0, BLOCKS + j - 1, 0) if j == 0 else unit_no(1, 0, 0))
                    split(j, n)
                with pool.Fori(1, BLOCKS // 2) as i:
                    for j in range(2):
                        pool.wait_ge(w_in[j], 16 * i + 16 * (BLOCKS * p // 2 + 1))
                        pool.wait_ge(unit_done, 2 * NT[p] * i + unit_no(p, j - 1, 0))
                        split(j, 2 * i + (BLOCKS * p + j))

        @block.tensor
        def _(pe):
            def half_unit(u, slot, hi, lo, c0, n, korder, half, ready=None, first=0):
                ps = bank[u % 4][:, 0:n]
                for j in range(4 * half, 4 * half + 4):
                    if ready is not None:
                        pe.wait_ge(ready, first + j)
                    kb = korder[j]
                    wh, wl = (w[:, slot, kb * P:(kb + 1) * P] for w in (w_hi, w_lo))
                    xh, xl = hi[:, kb, c0:c0 + n], lo[:, kb, c0:c0 + n]
                    pe.matmul(ps, wh, xh, start=(j == 0), stop=False)
                    pe.matmul(ps, wh, xl, start=False, stop=False)
                    mm = pe.matmul(ps, wl, xh, start=False, stop=(j == 7))
                if half:
                    mm.then_inc(unit_done, 1)

            def open_bank(a):
                if a >= 4:
                    drained(pe, a - 4)
                return aux[a % 4]

            def ones_sum(a, src, c0, n):
                pe.matmul(open_bank(a)[:, 0:n], ones[:, :], src[:, c0:c0 + n], start=True,
                          stop=True).then_inc(aux_done, 1)

            def final_sums(p):
                pe.wait_ge(f_sum, KB * sum(NT[:p + 1]))
                for t, (c0, w) in enumerate(TILES[p]):
                    ones_sum(AUX[(p, "NF", 0)] + t, rf, c0, w)

            def piece(p, name, i):
                a = AUX.get((p, name, i))
                n = 4 * p + i
                if name == "RS":
                    pe.wait_ge(consts, 5)
                    pe.wait_ge(const_in, 16 * 3)
                    pe.wait_ge(x_acc, KB * (p + 1))
                    for t, (c0, w) in enumerate(TILES[p]):
                        ones_sum(a + t, rs, c0, w)
                elif name == "NF":
                    final_sums(0)
                elif name == "VT":
                    for t in range(NT[p]):
                        evacuated(pe, unit_no(p, 5 * i + V, t))
                    for s, (c, m) in enumerate(chunk_sets(p)):
                        ps = open_bank(a + s)
                        for j in range(m):
                            lo_, hi_ = span(c + j)
                            mm = pe.transpose(ps[0:rows(c), j * P:(j + 1) * P], v[:, lo_:hi_], ident[:, :])
                        mm.then_inc(aux_done, 1)
                elif name == "D":
                    for t in range(NT[p]):
                        pe.wait_ge(post, post_no(p, 2, i, t) + 1)
                    for s, (c, m) in enumerate(chunk_sets(p)):
                        ps = open_bank(a + s)
                        for j in range(m):
                            lo_, hi_ = span(c + j)
                            mm = pe.matmul(ps[0:rows(c), j * P:j * P + rows(c)], k[:, lo_:hi_], q[:, lo_:hi_],
                                           start=True, stop=True)
                        mm.then_inc(aux_done, 1)
                elif name[0] == "L":
                    lv = int(name[1])
                    x = 1 << (lv - 1)
                    pe.wait_ge(level, 8 * n + lv)
                    ps = open_bank(a)
                    qv = q[:, 0:CH * NCH].rearrange("p (c n h x) -> p c n h x", c=NCH, h=2, x=x)
                    for c in range(NCH):
                        mm = pe.matmul(ps[:, 64 * c:64 * c + 64], k[:, CH * c:CH * c + CH], qv[:, c, :, 1, :],
                                       start=True, stop=True)
                    mm.then_inc(aux_done, 1)
                    if p and lv <= 4:
                        w = T8 if lv <= 2 else TAIL
                        q8 = q[:, CH * NCH:CH * NCH + w].rearrange("p (n h x) -> p n h x", h=2, x=x)
                        pe.matmul(open_bank(a + 1)[0:w, 0:w // 2], k[:, CH * NCH:CH * NCH + w], q8[:, :, 1, :],
                                  start=True, stop=True).then_inc(aux_done, 1)
                elif name == "KT":
                    pe.wait_ge(level, 8 * n + 8)
                    for s, (c, m) in enumerate(chunk_sets(p)):
                        ps = open_bank(a + s)
                        for j in range(m):
                            lo_, hi_ = span(c + j)
                            mm = pe.transpose(ps[0:rows(c), j * P:(j + 1) * P], k[:, lo_:hi_], ident[:, :])
                        mm.then_inc(aux_done, 1)
                elif name == "U":
                    for s in range(len(chunk_sets(p))):
                        drained(pe, AUX[(p, "VT", i)] + s)
                        drained(pe, AUX[(p, "KT", i)] + s)
                    for s, (c, m) in enumerate(chunk_sets(p)):
                        ps = open_bank(a + s)
                        for j in range(m):
                            r_ = CH if c < NCH else TAIL
                            mm = pe.matmul(ps[:, j * P:(j + 1) * P], k_tok[0:r_, c + j, :], v_tok[0:r_, c + j, :],
                                           start=True, stop=True)
                        mm.then_inc(aux_done, 1)
                    if p:
                        pe.wait_ge(s_step, s_at(p, i, "vm"))
                        for s in range(2):
                            pe.matmul(open_bank(a + 3 + s)[:, :], k_tok[0:T8, 8, :], tmp[0:T8, s, :],
                                      start=True, stop=True).then_inc(aux_done, 1)
                elif name == "O":
                    pe.wait_ge(s_step, s_at(p, i, "s7"))
                    if p:
                        drained(pe, AUX[(p, "U", i)] + 1)
                    for s, (c, m) in enumerate(chunk_sets(p)):
                        ps = open_bank(a + s)
                        for j in range(m):
                            lo_, hi_ = span(c + j)
                            out = ps[:, j * P:j * P + rows(c)]
                            if c < NCH:
                                pe.matmul(out, s_in[:, c + j, :], q[:, lo_:hi_], start=True, stop=False)
                                mm = pe.matmul(out, v_tok[:, c + j, :], attn[:, lo_:hi_], start=False, stop=True)
                                continue
                            pe.wait_ge(s_load, 16 * (i + 1))
                            pe.matmul(out, v_tok[0:T8, 8, :], attn[0:T8, lo_:hi_], start=True, stop=False,
                                      skip_group_check=True)
                            pe.matmul(ps[:, 0:TAIL], s_in[:, 8, :], q[:, lo_:lo_ + TAIL], start=False,
                                      stop=False, skip_group_check=True)
                            for b in range(NSEQ):
                                o_ = TAIL + SLEN * b
                                mm = pe.matmul(ps[:, o_:o_ + SLEN], s_smp[:, b, :],
                                               q[:, lo_ + o_:lo_ + o_ + SLEN], start=False,
                                               stop=(b == NSEQ - 1), skip_group_check=True)
                        mm.then_inc(aux_done, 1)
                elif name == "SS":
                    for s, (c, m) in enumerate(chunk_sets(p)):
                        drained(pe, AUX[(p, "O", i)] + s)
                        lo_, hi_ = span(c, m)
                        ones_sum(a + s, q, lo_, hi_ - lo_)
                elif name == "GATE":
                    pe.wait_ge(rg_step, rg_at(p, i, "sc3" if p else "c3"))
                    for t, (c0, w) in enumerate(TILES[p]):
                        for g, wt in enumerate((w_ra, w_rx)):
                            ps = open_bank(a + 2 * t + g)
                            pe.matmul(ps[:, 0:w], wt[:, i, :], xc[:, c0:c0 + w], start=True,
                                      stop=True).then_inc(aux_done, 1)

            def open_unit(u):
                if u >= 4:
                    evacuated(pe, u - 4)

            natural = list(range(KB))
            for p in range(2):
                nt = NT[p]
                for it, blk, t, half, pieces in schedule(p):
                    u = unit_no(p, blk, t)
                    c0, w = TILES[p][t]
                    if half == 0:
                        if t == 0:
                            pe.wait_ge(w_ready, BLOCKS * p + blk + 1)
                        open_unit(u)
                    half_unit(u, blk % 2, a_hi, a_lo, c0, w, natural, half, x_ready if blk == 0 else None,
                              tile_no(p, t, 0))
                    for name, i in pieces:
                        if name not in ("FN", "FY", "S1", "S2", "S3"):
                            piece(p, name, i)
                for m in range(KB):
                    blk = OUT0 + m
                    pe.wait_ge(w_ready, BLOCKS * p + blk + 1)
                    for t, (c0, w) in enumerate(TILES[p]):
                        u = unit_no(p, blk, t)
                        open_unit(u)
                        for half in range(2):
                            half_unit(u, blk % 2, a_hi, a_lo, c0, w, OUT_ORDER, half, y_ready if m == 0 else None,
                                      tile_no(p, t, 0))
                pe.wait_ge(b_sum, (KB - 1) * sum(NT[:p + 1]))
                for t, (c0, w) in enumerate(TILES[p]):
                    ones_sum(AUX[(p, "N2", 0)] + t, rs, c0, w)
                pe.wait_ge(b_lo_ready, KB * (nt + (NT[0] if p else 0)))
                hb = p * 8 * NT[0] * FF_GROUPS
                with pe.Fori(0, FF_GROUPS) as g:
                    for stage in range(2):
                        with pe.Fori(0, 2) as qd:
                            for j in range(4):
                                pe.wait_ge(w_ready, 16 * g + 4 * qd + (BLOCKS * p + MLP0 + 8 * stage + j + 1))
                                for t, (c0, w) in enumerate(TILES[p]):
                                    lu = j * nt + t
                                    pe.wait_ge(bank_free[lu % 4], 4 * nt * g + nt * qd
                                               + (unit_no(p, MLP0 + 8 * stage, 0) // 4 + lu // 4))
                                    if stage and j == 0:
                                        pe.wait_ge(h_ready, 8 * nt * g + (hb + 7 * nt + t + 1))
                                    hi, lo = (a_hi, a_lo) if stage else (b_hi, b_lo)
                                    for half in range(2):
                                        half_unit(lu, j % 2, hi, lo, c0, w, natural, half)
            final_sums(1)

        @block.scalar
        def _(act):
            def fn(out, in_, func, **kw):
                return nc.scalar.activation(out, in_, func, **kw)

            act.dma_start(par[:, :], par_d).then_inc(par_in, 16)

            def load_x(p, dst, b):
                x0 = TH[0] * p
                act.dma_start(dst[:, b, 0:TH[p]], xT[b, :, x0:x0 + TH[p]]).then_inc(x_in[b], 16)

            for t, (c0, w) in enumerate(TILES[0]):
                for b in range(KB):
                    act.dma_start(xs[:, b, c0:c0 + w], xT[b, :, c0:c0 + w]).then_inc((x_in2 if t else x_in)[b], 16)
            act.dma_start(ident[:, :], ident_d).then_inc(const_in, 16)
            act.dma_start(w_ra[:, :, :], wra_d).then_inc(const_in, 16)
            act.dma_start(w_rx[:, :, :], wrx_d).then_inc(const_in, 16)

            def store(p, b, c0, w):
                x0 = TH[0] * p
                act.dma_start(y_d[b, :, x0 + c0:x0 + c0 + w], xy[:, b, c0:c0 + w]).then_inc(stored, 16)

            def input_square(p, b):
                act.wait_ge(x_in[b], 16 * (2 * p + 1))
                if p == 0:
                    act.wait_ge(x_in2[b], 16)
                if b >= 2:
                    act.wait_ge(x_acc, KB * p + b - 1)
                fn(sq[b % 2][:, 0:TH[p]], xs[:, b, 0:TH[p]], ACT.Square).then_inc(x_sq, 1)

            def input_squares(p):
                for b in range(KB):
                    input_square(p, b)

            def load_small(p):
                act.dma_start(mask[:, :], mask_d).then_inc(smp_in, 16)
                if p == 0:
                    return
                act.dma_start(smask[:, :], smask_d).then_inc(smp_in, 16)
                act.dma_start(h0[:, :, :], h0_d).then_inc(smp_in, 16)
                act.dma_start(spad[:, :, :, 0:TAPS - 1], cs_d).then_inc(smp_in, 16)

            def load_state(i):
                act.dma_start(s_smp[:, :, :], ss_d[i]).then_inc(s_load, 16)

            def rms_tiles(p, a, dst):
                for t, (c0, w) in enumerate(TILES[p]):
                    filled(act, a + t)
                    fn(dst[:, c0:c0 + w], aux[(a + t) % 4][:, 0:w], ACT.Sqrt, bias=eps[:, 0:1],
                       scale=1.0 / DM).then_inc(aux_free[(a + t) % 4], 1)

            def piece(p, name, i):
                a = AUX.get((p, name, i))
                n = 4 * p + i
                if name == "RS":
                    act.wait_ge(consts, 5)
                    rms_tiles(p, a, rs)
                elif name == "NF":
                    rms_tiles(0, AUX[(0, "NF", 0)], rf)
                elif name == "FY":
                    act.wait_ge(y_out, i + 1)
                    store(0, i, 0, TH[0])
                elif name in ("VT", "KT"):
                    dst = v_tok if name == "VT" else k_tok
                    if name == "VT" and i > 0:
                        filled(act, AUX[(p, "O", i - 1)] + 1 + p)
                    if name == "KT" and i > 0:
                        filled(act, AUX[(p, "U", i - 1)] + aux_uses(p, "U") - 1)
                    if name == "KT":
                        act.wait_ge(rg_step, rg_at(p, i, "scan"))
                    for s, (c, m) in enumerate(chunk_sets(p)):
                        filled(act, a + s)
                        fn(dst[0:rows(c), c:c + m, :],
                           aux[(a + s) % 4][0:rows(c), 0:m * P].rearrange("p (c d) -> p c d", d=P),
                           ACT.Copy).then_inc(aux_free[(a + s) % 4], 1)
                elif name == "O":
                    filled(act, a + len(chunk_sets(p)) - 1)
                    if p and i == 0:
                        act.wait_ge(stored, 16 * KB)
                    for s, (c, m) in enumerate(chunk_sets(p)):
                        lo_, hi_ = span(c, m)
                        ps = aux[(a + s) % 4][:, 0:hi_ - lo_]
                        fn(xy[:, i, lo_:hi_], ps, ACT.Copy)
                        fn(q[:, lo_:hi_], ps, ACT.Square).then_inc(aux_free[(a + s) % 4], 1)
                    if p and i + 1 < HEADS:
                        act.wait_ge(s_step, s_at(p, i, "smul"))
                        load_state(i + 1)
                    if p:
                        for s in (3, 4):
                            drained(act, AUX[(p, "U", i)] + s)
                        act.dma_start(ssn_d[i], tmp[:, :, :]).then_inc(s_store, 16)
                elif name == "SS":
                    act.wait_ge(rg_step, rg_at(p, i, "scan"))
                    for s, (c, m) in enumerate(chunk_sets(p)):
                        lo_, hi_ = span(c, m)
                        filled(act, a + s)
                        fn(ea[:, lo_:hi_], aux[(a + s) % 4][:, 0:hi_ - lo_], ACT.Sqrt, bias=eps[:, 0:1],
                           scale=1.0 / P).then_inc(aux_free[(a + s) % 4], 1)
                elif name == "GATE":
                    if i > 0:
                        act.wait_ge(rg_step, rg_at(p, i - 1, "scan"))
                        filled(act, AUX[(p, "U", i - 1)] + aux_uses(p, "U") - 1)
                    for t, (c0, w) in enumerate(TILES[p]):
                        for g, (dst, b) in enumerate(((ta, "b_ra"), (ig, "b_rx"))):
                            u = a + 2 * t + g
                            filled(act, u)
                            fn(dst[:, c0:c0 + w], aux[u % 4][:, 0:w], ACT.Sigmoid,
                               bias=col(b, i)).then_inc(aux_free[u % 4], 1)
                    for t in range(NT[p]):
                        drained(act, a + 2 * t)
                    act.wait_ge(prep, PREP_STEPS)
                    if i > 0:
                        act.wait_ge(o_inv, O_STEPS * (n - 1) + 3)
                    fn(ea[:, 0:TH[p]], ta[:, 0:TH[p]], ACT.Exp, scale=sp[:, 3, i:i + 1])
                    fn(ta[:, 0:TH[p]], ta[:, 0:TH[p]], ACT.Tanh, scale=sp[:, 2, i:i + 1]).then_inc(rg_act, 1)
                    act.wait_ge(rg_step, rg_at(p, i, "v"))
                    fn(ea[:, 0:TH[p]], ea[:, 0:TH[p]], ACT.Sqrt, scale=-1.0).then_inc(rg_act, 1)

            def unit_fn(p, it, blk, t):
                u = unit_no(p, blk, t)
                c0, w = TILES[p][t]
                kind = blk - 5 * it if it < HEADS else None
                if kind in (G, Q):
                    pn = post_no(p, 0 if kind == G else 2, it, t)
                    evacuated(act, u)
                    if t >= 2:
                        act.wait_ge(post, pn - 1)
                    elif kind == Q:
                        act.wait_ge(post, post_no(p, 0, it, NT[p] - 1) + 1)
                        if p and it > 0:
                            act.wait_ge(s_store, 16 * it)
                    elif it > 0:
                        act.wait_ge(post, post_no(p, 2, it - 1, NT[p] - 1) + 1)
                    elif p:
                        act.wait_ge(f_sum, final_no(0, KB - 1, NT[0] - 1))
                    src = gate[:, it % 2, c0:c0 + w] if kind == G else q[:, c0:c0 + w]
                    fn(tmp[:, t % 2, 0:w], src, ACT.Sigmoid).then_inc(act_fn, 1)
                elif kind == F:
                    evacuated(act, u)
                    if it > 0:
                        filled(act, AUX[(p, "KT", it - 1)] + 1 + p)
                    fn(k[:, c0:c0 + w], f[:, c0:c0 + w], ACT.Sigmoid, scale=-1.0)
                    fn(f[:, c0:c0 + w], f[:, c0:c0 + w], ACT.Sigmoid).then_inc(act_fn, 1)
                elif kind is None:
                    evacuated(act, u)
                    fn(ge[:, c0:c0 + w], ge[:, c0:c0 + w], ACT.Gelu_apprx_tanh).then_inc(act_fn, 1)

            act.wait_ge(par_in, 16)
            act.wait_ge(prep, 3)
            fn(sp[:, 0, :], sp[:, 0, :], ACT.Exp, scale=-1.0).then_inc(prep_act, 1)
            fn(lbv[:, 0, :], lbv[:, 0, :], ACT.Exp).then_inc(prep_act, 1)

            for p in range(2):
                th = TH[p]
                for t, (c0, w) in enumerate(TILES[p]):
                    for b in range(KB):
                        if t == 0 or p == 0:
                            act.wait_ge((x_in2 if t else x_in)[b], 16 * (1 if t else 2 * p + 1))
                        if p and b == 0 and t == 0:
                            act.wait_ge(unit_done, unit_no(1, 0, 0))
                        fn(a_hi[:, b, c0:c0 + w], xs[:, b, c0:c0 + w], ACT.Copy,
                           scale=col("ln_mix", b)).then_inc(x_hi, 1)
                if p == 0:
                    input_squares(0)
                act.wait_ge(x_acc, KB * p + KB)
                act.wait_ge(x_ready, tile_no(p, NT[p] - 1, KB - 1))
                load_small(p)
                if p:
                    load_state(0)
                queue = []
                started = False
                for it, blk, t, half, pieces in schedule(p):
                    if ("RS", 0) in pieces:
                        piece(p, "RS", 0)
                        started = True
                    if half:
                        queue.append((it, blk, t))
                    while started and queue:
                        unit_fn(p, *queue.pop(0))
                    for name, i in pieces:
                        if name not in ("RS", "FN", "S1", "S2", "S3"):
                            piece(p, name, i)
                if p:
                    act.wait_ge(rg_step, rg_at(1, 3, "ncs"))
                    act.dma_start(hs_d, hout[:, :, :]).then_inc(small_out, 16)
                    act.dma_start(csn_d, ncs[:, :, :, :]).then_inc(small_out, 16)
                act.wait_ge(unit_done, unit_no(p, OUT0, 0))
                for t, (c0, w) in enumerate(TILES[p]):
                    for n, b in enumerate(OUT_ORDER):
                        if b < HEADS:
                            act.wait_ge(o_inv, O_STEPS * (4 * p + b) + O_STEPS)
                        else:
                            act.wait_ge(post, post_no(p, 3, b - HEADS, NT[p] - 1) + 1)
                        fn(a_hi[:, b, c0:c0 + w], xy[:, b, c0:c0 + w], ACT.Copy).then_inc(y_hi, 1)
                for n, b in enumerate(OUT_ORDER):
                    act.wait_ge(y_ready, tile_no(p, NT[p] - 1, n))
                    load_x(p, xy, b)
                if p:
                    act.wait_ge(small_out, 16 * 2)
                    act.wait_ge(s_store, 16 * HEADS)
                for m in range(KB):
                    for t, (c0, w) in enumerate(TILES[p]):
                        u = unit_no(p, OUT0 + m, t)
                        bu = KB * NT[0] * p + m * NT[p] + t
                        evacuated(act, u)
                        fn(b_hi[:, m, c0:c0 + w], xy[:, m, c0:c0 + w], ACT.Copy, scale=col("ln_mlp", m))
                        if m == 0:
                            dst = rs[:, c0:c0 + w]
                        else:
                            dst = tmp[:, bu % 2, 0:w]
                            if m * NT[p] + t - 2 >= NT[p]:
                                act.wait_ge(b_sum, sum_no(p, m, t) - 2)
                        fn(dst, xy[:, m, c0:c0 + w], ACT.Square).then_inc(b_act, 1)
                rms_tiles(p, AUX[(p, "N2", 0)], rs)
                nt = NT[p]
                ub = unit_no(p, MLP0, 0) // 4

                def squared_relu(g, qd):
                    for j in range(4):
                        for t, (c0, w) in enumerate(TILES[p]):
                            lu = j * nt + t
                            act.wait_ge(bank_free[lu % 4], 4 * nt * g + nt * qd + (ub + lu // 4 + 1))
                            z = tmp[:, lu % 2, 0:w]
                            fn(a_hi[:, 4 * qd + j, c0:c0 + w], z, ACT.Square)
                            fn(z, z, ACT.Square).then_inc(h_sq, 1)

                with act.Fori(0, FF_GROUPS - 1) as g:
                    with act.Fori(0, 2) as qd:
                        squared_relu(g, qd)
                for qd in range(2):
                    squared_relu(FF_GROUPS - 1, qd)
                if p == 0:
                    act.wait_ge(unit_done, unit_no(0, BLOCKS - KB, 0))
                    for b in range(KB):
                        load_x(1, xs, b)
                act.wait_ge(h_ready, 8 * FF_GROUPS * sum(NT[:p + 1]))
                for m in range(KB):
                    for t, (c0, w) in enumerate(TILES[p]):
                        evacuated(act, unit_no(p, BLOCKS - KB + m, t))
                        if m * nt + t >= 2:
                            act.wait_ge(f_sum, final_no(p, m, t) - 2)
                        fn(tmp[:, (m * nt + t) % 2, 0:w], xy[:, m, c0:c0 + w], ACT.Square).then_inc(f_sq, 1)
                    if p == 0:
                        for b in SQUARES_AFTER.get(m, []):
                            input_square(1, b)
            rms_tiles(1, AUX[(1, "NF", 0)], rf)
            for t, (c0, w) in enumerate(TILES[1]):
                for b in range(KB):
                    act.wait_ge(y_out, KB + KB * t + b + 1)
                    store(1, b, c0, w)
            act.wait_ge(rg_step, rg_at(1, 3, "ncs"))
            act.dma_start(hp_d, hprev[:, :]).then_inc(small_out, 16)
            act.dma_start(cp_d, xhist[:, :, :]).then_inc(small_out, 16)
            drained(act, AUX[(1, "U", 3)] + 2)
            act.dma_start(sp_d, state[:, :, :]).then_inc(small_out, 16)
            act.wait_ge(small_out, 16 * 5)
            act.wait_ge(s_store, 16 * HEADS)
            act.wait_ge(stored, 16 * KB * (1 + NT[1]))

        @block.vector
        def _(dve):
            tt, ts, stt = dve.tensor_tensor, dve.tensor_scalar, dve.scalar_tensor_tensor
            count = {"prep": 0}

            def prep_step(ins):
                count["prep"] += 1
                ins.then_inc(prep, 1)
                dve.wait_ge(prep, count["prep"])

            def rg(p, i, name, ins):
                ins.then_inc(rg_step, 1)
                dve.wait_ge(rg_step, rg_at(p, i, name))

            def invert_tile(p, a, t, dst):
                c0, w = TILES[p][t]
                drained(dve, a + t)
                dve.reciprocal(dst[:, c0:c0 + w], dst[:, c0:c0 + w]).then_inc(rf_ready if dst is rf else rs_ready, 1)

            def invert(p, which, a):
                for t in range(NT[p]):
                    invert_tile(p, a, t, rs)
                dve.wait_ge(rs_ready, norms_before(p, which) + NT[p])

            def scale_out(p, b, c0, w):
                y = xy[:, b, c0:c0 + w]
                stt(y, y, col("ln_final", b), rf[:, c0:c0 + w], ALU.mult, ALU.mult).then_inc(y_out, 1)

            def add_input_square(p, b):
                th = TH[p]
                dve.wait_ge(x_sq, KB * p + b + 1)
                if b == 0:
                    ins = dve.tensor_copy(rs[:, 0:th], sq[0][:, 0:th])
                else:
                    dve.wait_ge(x_acc, KB * p + b)
                    ins = tt(rs[:, 0:th], rs[:, 0:th], sq[b % 2][:, 0:th], ALU.add)
                ins.then_inc(x_acc, 1)

            def merge(p, head, lv):
                x = 1 << (lv - 1)
                n = TH[p] if lv <= 2 else (NP[p] if lv <= 4 else CH * NCH)
                qv, kv, fv = (b[:, 0:n].rearrange("p (n h x) -> p n h x", h=2, x=x) for b in (q, k, f))
                left, right = fv[:, :, 0, x - 1:x], fv[:, :, 1, x - 1:x]
                shape = [P, n // (2 * x), x]
                tt(qv[:, :, 1, :], qv[:, :, 1, :], left.broadcast_to(shape), ALU.mult)
                tt(kv[:, :, 0, :], kv[:, :, 0, :], right.broadcast_to(shape), ALU.mult).then_inc(spread, 1)
                dve.wait_ge(spread, LEVELS * head + lv)
                return tt(right, right, left, ALU.mult)

            def place(p, lv, a):
                if lv == 0:
                    for s, (c, m) in enumerate(chunk_sets(p)):
                        filled(dve, a + s)
                        r_ = rows(c)
                        lo_, hi_ = span(c, m)
                        mk = mask[0:r_, 0:r_].rearrange("p (o t) -> p o t", o=1).broadcast_to([r_, m, r_])
                        dve.copy_predicated(attn[0:r_, lo_:hi_].rearrange("p (c t) -> p c t", c=m), mk,
                                            aux[(a + s) % 4][0:r_, 0:m * r_].rearrange(
                                                "p (c t) -> p c t", c=m)).then_inc(aux_free[(a + s) % 4], 1)
                    return
                x = 1 << (lv - 1)
                m0 = P + 64 * (lv - 1)
                parts = [(a, P, 0, CH * NCH, NCH)]
                if p and lv <= 4:
                    w = T8 if lv <= 2 else TAIL
                    parts.append((a + 1, w, CH * NCH, CH * NCH + w, 1))
                for u, r_, lo_, hi_, nc_ in parts:
                    filled(dve, u)
                    w = (hi_ - lo_) // nc_ // 2
                    dst = attn[0:r_, lo_:hi_].rearrange("p (c n h x) -> p c n h x", c=nc_, h=2, x=x)[:, :, :, 1, :]
                    src = aux[u % 4][0:r_, 0:w * nc_].rearrange("p (c n x) -> p c n x", c=nc_, x=x)
                    mk = mask[0:r_, m0:m0 + w].rearrange("p (o n x) -> p o n x", o=1, x=x)
                    dve.copy_predicated(dst, mk.broadcast_to([r_, nc_, w // x, x]), src).then_inc(aux_free[u % 4], 1)

            def piece(p, name, i):
                a = AUX.get((p, name, i))
                n = 4 * p + i
                th = TH[p]
                if name == "RS":
                    invert(p, 0, a)
                elif name == "FN":
                    invert_tile(0, AUX[(0, "NF", 0)], i, rf)
                elif name == "FY":
                    dve.wait_ge(rf_ready, NT[0])
                    scale_out(0, i, 0, TH[0])
                elif name == "D":
                    if i > 0:
                        filled(dve, AUX[(p, "O", i - 1)] + 1 + p)
                    place(p, 0, a)
                    dve.wait_ge(post, post_no(p, 2, i, NT[p] - 1) + 1)
                    tt(q[:, 0:th], q[:, 0:th], f[:, 0:th], ALU.mult).then_inc(level, 1)
                elif name[0] == "L":
                    lv = int(name[1])
                    dve.wait_ge(level, 8 * n + lv)
                    place(p, lv, a)
                    merge(p, n, lv).then_inc(level, 1)
                elif name == "KT" and p:
                    drained(dve, AUX[(p, "VT", i)] + 2)
                    if i > 0:
                        dve.wait_ge(s_store, 16 * i)
                    dve.wait_ge(post, post_no(p, 0, min(i + 1, HEADS - 1), NT[p] - 1) + 1)
                    vm = tmp[0:T8, :, :].rearrange("p a (b d) -> p (a b) d", d=P)
                    tt(vm, v_tok[0:T8, 8:9, :].broadcast_to([T8, NSEQ, P]),
                       smask[0:T8, :].rearrange("p (b o) -> p b o", o=1).broadcast_to([T8, NSEQ, P]),
                       ALU.mult).then_inc(s_step, 1)
                elif name == "U":
                    dve.wait_ge(level, 8 * n + 8)
                    if i > 0:
                        filled(dve, AUX[(p, "O", i - 1)] + 1 + p)
                    dve.tensor_copy(s_in[:, 0, :], state[:, i, :]).then_inc(s_step, 1)
                    last = NCH + p
                    for c in range(last):
                        u = a + c // 4
                        filled(dve, u)
                        if c % 4 == 0 and c:
                            drained(dve, u - 1)
                        else:
                            dve.wait_ge(s_step, s_at(p, i, f"s{c}"))
                        end = CH * c + (CH if c < NCH else TAIL) - 1
                        dst = s_in[:, c + 1, :] if c + 1 < last else state[:, i, :]
                        ins = stt(dst, s_in[:, c, :], f[:, end:end + 1],
                                  aux[u % 4][:, (c % 4) * P:(c % 4 + 1) * P], ALU.mult, ALU.add)
                        if c % 4 == 3 or c == NCH:
                            ins.then_inc(aux_free[u % 4], 1)
                        else:
                            ins.then_inc(s_step, 1)
                    if p:
                        filled(dve, a + 4)
                        dve.wait_ge(s_load, 16 * (i + 1))
                        tot = f[:, NP[1] + SLEN - 1:TH[1]:SLEN].rearrange("p (b o) -> p b o", o=1)
                        new = tmp[:, :, :].rearrange("p a (b d) -> p (a b) d", d=P)
                        tt(new, s_smp[:, :, :], tot.broadcast_to([P, NSEQ, P]), ALU.mult).then_inc(s_step, 1)
                        dve.wait_ge(s_step, s_at(p, i, "smul"))
                        for s in range(2):
                            tt(tmp[:, s, :], tmp[:, s, :], aux[(a + 3 + s) % 4][:, :], ALU.add).then_inc(
                                aux_free[(a + 3 + s) % 4], 1)
                elif name in ("S1", "S2"):
                    lo_, hi_ = (0, 4 * CH) if name == "S1" else (4 * CH, th)
                    for s in ([0] if name == "S1" else range(1, 2 + p)):
                        drained(dve, AUX[(p, "SS", i)] + s)
                    dve.reciprocal(ea[:, lo_:hi_], ea[:, lo_:hi_]).then_inc(o_inv, 1)
                elif name == "S3":
                    dve.wait_ge(o_inv, O_STEPS * n + 2)
                    y = xy[:, i, 0:th]
                    stt(y, y, col("gn"), ea[:, 0:th], ALU.mult, ALU.mult).then_inc(o_inv, 1)
                    dve.wait_ge(o_inv, O_STEPS * n + 3)
                    tt(y, y, gate[:, i % 2, 0:th], ALU.mult).then_inc(o_inv, 1)
                elif name == "GATE":
                    dve.wait_ge(rg_act, 2 * n + 1)
                    T, E, I = ta[:, 0:th], ea[:, 0:th], ig[:, 0:th]
                    rg(p, i, "u", stt(E, E, 1.0, T, ALU.add, ALU.mult))
                    rg(p, i, "a", ts(T, E, -1.0, 1.0, ALU.mult, ALU.add))
                    rg(p, i, "v", stt(E, E, 2.0, E, ALU.subtract, ALU.mult))
                    for t in range(NT[p]):
                        drained(dve, a + 2 * t + 1)
                    rg(p, i, "igx", tt(I, I, xc[:, 0:th], ALU.mult))
                    dve.wait_ge(rg_act, 2 * n + 2)
                    rg(p, i, "bt", tt(I, I, E, ALU.mult))
                    if p:
                        first = slice(NP[1], TH[1], SLEN)
                        rg(p, i, "fold", tt(fold[:, :], ta[:, first], h0[:, i, :], ALU.mult))
                        rg(p, i, "foldadd", tt(ig[:, first], ig[:, first], fold[:, :], ALU.add))
                        rg(p, i, "cut", dve.memset(ta[:, first], 0.0))
                    y = xy[:, HEADS + i, :]
                    if p and i == 0:
                        dve.wait_ge(stored, 16 * KB)
                    rg(p, i, "scan", dve.tensor_tensor_scan(y[:, 0:th], T, I, hprev[:, i:i + 1], ALU.mult, ALU.add))
                    rg(p, i, "hprev", dve.tensor_copy(hprev[:, i:i + 1], y[:, NP[p] - 1:NP[p]]))
                    rg(p, i, "xhist", dve.tensor_copy(xhist[:, i, :], xpad[:, NP[p]:NP[p] + TAPS - 1]))
                    if p:
                        rg(p, i, "hout", dve.tensor_copy(hout[:, i, :], y[:, NP[1] + SLEN - 1:TH[1]:SLEN]))
                        rg(p, i, "ncs", dve.tensor_copy(ncs[:, i, :, :], spad[:, i, :, SLEN:SLEN + TAPS - 1]))

            def read_out(p, it, blk, t):
                u = unit_no(p, blk, t)
                c0, w = TILES[p][t]
                kind = blk - 5 * it if it < HEADS else None
                ps = bank[u % 4]
                if kind == V and it > 0:
                    filled(dve, AUX[(p, "VT", it - 1)] + 1 + p)
                if kind == Q and it > 0:
                    filled(dve, AUX[(p, "SS", it - 1)] + 1 + p)
                if p and kind == G and it == 1:
                    dve.wait_ge(y_out, KB)
                if kind is None and blk > GA0:
                    dve.wait_ge(post, post_no(p, 3, blk - GA0 - 1, t) + 1)
                dve.wait_ge(unit_done, u + 1)
                if kind == XA and c0 + w > NP[p]:
                    n = NP[p] - c0
                    tt(xpad[:, TAPS - 1 + c0:TAPS - 1 + NP[p]], ps[:, 0:n], rs[:, c0:c0 + n], ALU.mult)
                    tt(spad[:, it, :, TAPS - 1:], ps[:, n:w].rearrange("p (b s) -> p b s", s=SLEN),
                       rs[:, NP[p]:c0 + w].rearrange("p (b s) -> p b s", s=SLEN),
                       ALU.mult).then_inc(bank_free[u % 4], 1)
                    return
                dst = {V: v[:, c0:c0 + w], G: gate[:, it % 2, c0:c0 + w], F: f[:, c0:c0 + w], Q: q[:, c0:c0 + w],
                       XA: xpad[:, TAPS - 1 + c0:min(TAPS - 1 + c0 + w, TAPS - 1 + NP[p])], None: ge[:, c0:c0 + w]}[kind]
                tt(dst, ps[:, 0:w], rs[:, c0:c0 + w], ALU.mult).then_inc(bank_free[u % 4], 1)

            def finish_unit(p, it, blk, t):
                c0, w = TILES[p][t]
                kind = blk - 5 * it if it < HEADS else None
                if kind in (V, XA):
                    return
                pn = post_no(p, {G: 0, F: 1, Q: 2, None: 3}[kind], it if it < HEADS else blk - GA0, t)
                dve.wait_ge(act_fn, pn + 1)
                z = tmp[:, t % 2, 0:w]
                if kind == G:
                    d = gate[:, it % 2, c0:c0 + w]
                    tt(d, d, z, ALU.mult).then_inc(post, 1)
                elif kind == Q:
                    stt(q[:, c0:c0 + w], q[:, c0:c0 + w], QSCALE, z, ALU.mult, ALU.mult).then_inc(post, 1)
                elif kind == F:
                    fc, kc = f[:, c0:c0 + w], k[:, c0:c0 + w]
                    if p == 0 and it == 0 and t == 0:
                        dve.wait_ge(prep, PREP_STEPS)
                    ts(fc, fc, lbv[:, 1, it:it + 1], lbv[:, 0, it:it + 1], ALU.mult, ALU.add).then_inc(post_half, 1)
                    ts(kc, kc, lbv[:, 1, it:it + 1], None, ALU.mult)
                    dve.wait_ge(post_half, (p * 4 * NT[0]) + it * NT[p] + t + 1)
                    ts(fc, fc, F_MIN, None, ALU.max).then_inc(post, 1)
                else:
                    c = blk - GA0
                    y = xy[:, HEADS + c, c0:c0 + w]
                    tt(y, y, ge[:, c0:c0 + w], ALU.mult).then_inc(post, 1)

            def convolve(p, i):
                for t in range(NT[p]):
                    evacuated(dve, unit_no(p, 5 * i + XA, t))
                rg(p, i, "hist", dve.tensor_copy(xpad[:, 0:TAPS - 1], xhist[:, i, :]))

                def taps(out, src, names):
                    for j, name in enumerate(names):
                        wj = col("conv_w", 4 * i + j)
                        if j == 0:
                            rg(p, i, name, ts(out, src(0), wj, col("conv_b", i), ALU.mult, ALU.add))
                        else:
                            rg(p, i, name, stt(out, src(j), wj, out, ALU.mult, ALU.add))

                taps(xc[:, 0:NP[p]], lambda j: xpad[:, j:j + NP[p]], ["c0", "c1", "c2", "c3"])
                if p:
                    taps(xc[:, NP[1]:TH[1]].rearrange("p (b s) -> p b s", s=SLEN),
                         lambda j: spad[:, i, :, j:j + SLEN], ["sc0", "sc1", "sc2", "sc3"])

            lam = par[:, PC["lam"]:PC["lam"] + 4]
            lb_in = par[:, PC["lb"]:PC["lb"] + 4]
            dve.wait_ge(par_in, 16)
            prep_step(ts(sp[:, 1, :], lam, -1.0, None, ALU.mult))
            prep_step(tt(sp[:, 0, :], sp[:, 1, :], lam, ALU.max))
            prep_step(tt(lbv[:, 0, :], lb_in, lb_in, ALU.subtract))

            def rest_of_prep():
                dve.wait_ge(prep_act, 2)
                prep_step(dve.reciprocal(lbv[:, 1, :], lbv[:, 0, :]))
                prep_step(tt(lbv[:, 0, :], lbv[:, 0, :], lbv[:, 1, :], ALU.mult))
                prep_step(tt(lbv[:, 0, :], lbv[:, 0, :], lbv[:, 0, :], ALU.subtract))
                prep_step(ts(lbv[:, 0, :], lbv[:, 0, :], 0.0, 1.0, ALU.max, ALU.min))
                prep_step(ts(lbv[:, 1, :], lbv[:, 0, :], -1.0, 1.0, ALU.mult, ALU.add))
                prep_step(ts(sp[:, 2, :], sp[:, 0, :], 2.0, None, ALU.add))
                prep_step(dve.reciprocal(sp[:, 2, :], sp[:, 2, :]))
                prep_step(tt(sp[:, 0, :], sp[:, 0, :], sp[:, 2, :], ALU.mult))
                prep_step(tt(sp[:, 2, :], sp[:, 0, :], sp[:, 0, :], ALU.mult))
                prep_step(ts(sp[:, 3, :], sp[:, 2, :], 1.0 / 17, None, ALU.mult))
                for d in (15, 13, 11, 9, 7, 5, 3):
                    prep_step(stt(sp[:, 3, :], sp[:, 3, :], 1.0 / d, sp[:, 2, :], ALU.add, ALU.mult))
                prep_step(stt(sp[:, 3, :], sp[:, 3, :], 1.0, sp[:, 0, :], ALU.add, ALU.mult))
                prep_step(ts(sp[:, 3, :], sp[:, 3, :], 2.0, None, ALU.mult))
                prep_step(stt(sp[:, 1, :], sp[:, 1, :], 0.0, sp[:, 3, :], ALU.max, ALU.add))
                prep_step(ts(sp[:, 2, :], sp[:, 1, :], 4.0, None, ALU.mult))
                prep_step(ts(sp[:, 3, :], sp[:, 1, :], -8.0, None, ALU.mult))
                assert count["prep"] == PREP_STEPS

            for p in range(2):
                th, nt = TH[p], NT[p]
                for t, (c0, w) in enumerate(TILES[p]):
                    for b in range(KB):
                        dve.wait_ge(x_hi, tile_no(p, t, b))
                        stt(a_lo[:, b, c0:c0 + w], xs[:, b, c0:c0 + w], col("ln_mix", b),
                            a_hi[:, b, c0:c0 + w].bitcast(F32), ALU.mult, ALU.subtract).then_inc(x_ready, 1)
                if p == 0:
                    for b in range(KB):
                        add_input_square(0, b)
                    rest_of_prep()
                dve.wait_ge(x_ready, tile_no(p, NT[p] - 1, KB - 1))
                dve.memset(attn[:, :], 0.0).then_inc(zeroed, 1)
                dve.wait_ge(zeroed, p + 1)
                dve.wait_ge(smp_in, 16 * (1 + 4 * p))
                dve.wait_ge(consts, 5)
                pending = []
                queue = []
                started = False
                for it, blk, t, half, pieces in schedule(p):
                    names = [n_ for n_, _ in pieces]
                    if "RS" in names:
                        piece(p, "RS", 0)
                        started = True
                    if half:
                        queue.append((it, blk, t))
                    while started and queue:
                        un = queue.pop(0)
                        read_out(p, *un)
                        if un[1] == 5 * un[0] + XA and un[0] < HEADS and un[2] == nt - 1:
                            convolve(p, un[0])
                        pending.append(un)
                        if len(pending) > 1:
                            finish_unit(p, *pending.pop(0))
                    last_of_iteration = half and t == nt - 1 and blk in (5 * it + Q, GA0 + 3)
                    if last_of_iteration:
                        while pending:
                            finish_unit(p, *pending.pop(0))
                    for name, i in pieces:
                        if name not in ("RS", "NF"):
                            piece(p, name, i)
                for t, (c0, w) in enumerate(TILES[p]):
                    for n, b in enumerate(OUT_ORDER):
                        dve.wait_ge(y_hi, tile_no(p, t, n))
                        tt(a_lo[:, b, c0:c0 + w], xy[:, b, c0:c0 + w], a_hi[:, b, c0:c0 + w].bitcast(F32),
                           ALU.subtract).then_inc(y_ready, 1)
                for m in range(KB):
                    dve.wait_ge(x_in[m], 16 * (2 * p + 2))
                    for t, (c0, w) in enumerate(TILES[p]):
                        u = unit_no(p, OUT0 + m, t)
                        bu = KB * NT[0] * p + m * nt + t
                        x = xy[:, m, c0:c0 + w]
                        dve.wait_ge(unit_done, u + 1)
                        tt(x, x, bank[u % 4][:, 0:w], ALU.add).then_inc(bank_free[u % 4], 1)
                        dve.wait_ge(b_act, bu + 1)
                        stt(b_lo[:, m, c0:c0 + w], x, col("ln_mlp", m), b_hi[:, m, c0:c0 + w].bitcast(F32),
                            ALU.mult, ALU.subtract).then_inc(b_lo_ready, 1)
                        if m:
                            if m > 1:
                                dve.wait_ge(b_sum, sum_no(p, m - 1, t))
                            r_ = rs[:, c0:c0 + w]
                            tt(r_, r_, tmp[:, bu % 2, 0:w], ALU.add).then_inc(b_sum, 1)
                invert(p, 1, AUX[(p, "N2", 0)])
                ub = unit_no(p, MLP0, 0)
                hb = p * 8 * NT[0] * FF_GROUPS

                def hidden(g, qd):
                    for j in range(4):
                        for t, (c0, w) in enumerate(TILES[p]):
                            lu = j * nt + t
                            dve.wait_ge(unit_done, 16 * nt * g + 4 * nt * qd + (ub + lu + 1))
                            z = tmp[:, lu % 2, 0:w]
                            stt(z, bank[lu % 4][:, 0:w], 0.0, rs[:, c0:c0 + w], ALU.max,
                                ALU.mult).then_inc(bank_free[lu % 4], 1)
                            dve.wait_ge(h_sq, 8 * nt * g + 4 * nt * qd + (hb + lu + 1))
                            tt(a_lo[:, 4 * qd + j, c0:c0 + w], z, a_hi[:, 4 * qd + j, c0:c0 + w].bitcast(F32),
                               ALU.subtract).then_inc(h_ready, 1)

                def add_residual(g, qd, j, t):
                    c0, w = TILES[p][t]
                    lu = j * nt + t
                    dve.wait_ge(unit_done, 16 * nt * g + 4 * nt * qd + (ub + 8 * nt + lu + 1))
                    x = xy[:, 4 * qd + j, c0:c0 + w]
                    tt(x, x, bank[lu % 4][:, 0:w], ALU.add).then_inc(bank_free[lu % 4], 1)

                with dve.Fori(0, FF_GROUPS - 1) as g:
                    with dve.Fori(0, 2) as qd:
                        hidden(g, qd)
                    with dve.Fori(0, 2) as qd:
                        for j in range(4):
                            for t in range(nt):
                                add_residual(g, qd, j, t)
                for qd in range(2):
                    hidden(FF_GROUPS - 1, qd)
                dve.wait_ge(h_ready, 8 * FF_GROUPS * sum(NT[:p + 1]))
                for m in range(KB):
                    for t, (c0, w) in enumerate(TILES[p]):
                        add_residual(FF_GROUPS - 1, m // 4, m % 4, t)
                        dve.wait_ge(f_sq, final_no(p, m, t))
                        r_, z = rf[:, c0:c0 + w], tmp[:, (m * nt + t) % 2, 0:w]
                        if m == 0:
                            ins = dve.tensor_copy(r_, z)
                        else:
                            dve.wait_ge(f_sum, final_no(p, m - 1, t))
                            ins = tt(r_, r_, z, ALU.add)
                        ins.then_inc(f_sum, 1)
                    if p == 0:
                        for b in SQUARES_AFTER.get(m, []):
                            add_input_square(1, b)
            for t, (c0, w) in enumerate(TILES[1]):
                invert_tile(1, AUX[(1, "NF", 0)], t, rf)
                dve.wait_ge(rf_ready, NT[0] + t + 1)
                for b in range(KB):
                    scale_out(1, b, c0, w)


def _weight_blocks(w_in, w_out, w_up, w_down):
    def blk(w, r0, c0):
        return w[r0:r0 + DM, c0:c0 + P].reshape(KB, P, P).transpose(1, 0, 2).reshape(P, DM)

    half = DM // 2
    xa0, ga0, q0, f0, v0, g0 = (half * j for j in range(6))
    out = []
    for i in range(HEADS):
        out += [blk(w_in, 0, c + P * i) for c in (v0, g0, xa0, f0, q0)]
    out += [blk(w_in, 0, ga0 + P * c) for c in range(4)]
    w_o = np.concatenate([w_out[half:], w_out[:half]], axis=0)
    out += [blk(w_o, 0, P * m) for m in range(KB)]
    for g in range(FF_GROUPS):
        out += [blk(w_up, 0, DM * g + P * m) for m in range(KB)]
        out += [blk(w_down, DM * g, P * m) for m in range(KB)]
    return np.stack(out)


def _masks():
    s = np.arange(P)[:, None]
    out = [(s == np.arange(P)[None, :])]
    j = np.arange(64)[None, :]
    for lv in range(1, LEVELS + 1):
        x = 1 << (lv - 1)
        t = (j // x) * 2 * x + x + j % x
        out.append((s // (2 * x) == t // (2 * x)) & (s % (2 * x) < x))
    return np.concatenate(out, axis=1).astype(np.int32)


def kernel(x_prompt, x_sample, state_rglru_h, state_rglru_conv, state_hgrn2, meta_tokens, ln_mix, w_in, conv_w,
           conv_b, w_rg_a, b_rg_a, w_rg_x, b_rg_x, rg_lambda, hgrn_lb, hgrn_norm, w_out, ln_mlp, w_up, w_down,
           ln_final):
    import concourse.bacc as bacc
    from concourse.bass_utils import run_bass_kernel_spmd

    A = np.asarray
    x = np.concatenate([A(meta_tokens), A(x_prompt)[0], A(x_sample).reshape(NSMP, DM)], axis=0)
    cols = lambda a, n: A(a).reshape(n, P).T

    def diagonal(w):
        w = A(w)[0]
        out = np.zeros((P, 4, P), w.dtype)
        for h in range(8):
            r0 = 64 * (h % 2)
            out[r0:r0 + 64, h // 2, r0:r0 + 64] = w[h]
        return out

    taps = A(conv_w)[0].reshape(TAPS, 4, P).transpose(2, 1, 0).reshape(P, 16)
    params = np.concatenate([cols(ln_mix, 8), cols(ln_mlp, 8), cols(ln_final, 8), taps, cols(conv_b, 4),
                             cols(b_rg_a, 4), cols(b_rg_x, 4), cols(rg_lambda, 4), cols(hgrn_lb, 4),
                             A(hgrn_norm).reshape(P, 1)], axis=1)
    smask = np.zeros((T8, NSEQ), np.float32)
    for b in range(NSEQ):
        smask[TAIL + SLEN * b:TAIL + SLEN * (b + 1), b] = 1.0
    arrays = {
        "xT": x.T.reshape(KB, P, x.shape[0]),
        "wall": _weight_blocks(A(w_in)[0], A(w_out)[0], A(w_up)[0], A(w_down)[0]),
        "params": params,
        "w_ra": diagonal(w_rg_a),
        "w_rx": diagonal(w_rg_x),
        "h0": A(state_rglru_h)[0].reshape(NSEQ, 4, P).transpose(2, 1, 0),
        "conv0": A(state_rglru_conv)[0].reshape(NSEQ, TAPS - 1, 4, P).transpose(3, 2, 0, 1),
        "state0": A(state_hgrn2)[0].transpose(1, 2, 0, 3),
        "ident": np.eye(P, dtype=np.float32),
        "mask": _masks(),
        "smask": smask,
    }
    outs = {"y": (KB, P, x.shape[0]), "hp": (P, 4), "cp": (P, 4, TAPS - 1), "sp_out": (P, HEADS, P),
            "hs": (P, 4, NSEQ), "csn": (P, 4, NSEQ, TAPS - 1), "ssn": (HEADS, P, NSEQ, P)}

    nc = bacc.Bacc("TRN2", target_bir_lowering=False, num_devices=1)
    arrays = {n: np.ascontiguousarray(a) for n, a in arrays.items()}
    ins = [nc.dram_tensor(f"in_{n}", a.shape, mybir.dt.from_np(a.dtype), kind="ExternalInput").ap()
           for n, a in arrays.items()]
    outputs = [nc.dram_tensor(f"out_{n}", s, F32, kind="ExternalOutput").ap() for n, s in outs.items()]
    build(nc, ins, outputs)
    r = run_bass_kernel_spmd(nc, [{f"in_{n}": a for n, a in arrays.items()}], core_ids=[0])
    y, hp, cp, sp, hs, csn, ssn = (r.results[0][f"out_{n}"] for n in outs)

    yt = y.reshape(DM, -1).T
    return (yt[META:META + SEQ].reshape(1, SEQ, DM),
            yt[META + SEQ:].reshape(NSEQ, SLEN, DM),
            hp.T.reshape(1, 1, DM // 2),
            cp.transpose(2, 1, 0).reshape(1, 1, TAPS - 1, DM // 2),
            sp.transpose(1, 0, 2).reshape(1, 1, HEADS, P, P),
            hs.transpose(2, 1, 0).reshape(1, NSEQ, DM // 2),
            csn.transpose(2, 3, 1, 0).reshape(1, NSEQ, TAPS - 1, DM // 2),
            ssn.transpose(2, 0, 1, 3).reshape(1, NSEQ, HEADS, P, P))
```
